# Optimizing a Trainium2 kernel written in Bass

```python
import jax, jax.numpy as jnp
from jax import lax
import numpy as np

D_MODEL = 2048
BATCH = 1
SEQ = 256
DEPTH = 2

HEAD_DIM = 128
D_MIX = D_MODEL
CONV_WIDTH = D_MIX // 2
POOL_WIDTH = D_MIX // 4
FOURIER_WIDTH = D_MIX // 4
POOL_WINDOWS = (2, 4, 8, 16)
POOL_GROUP = POOL_WIDTH // len(POOL_WINDOWS)
FOURIER_HEADS = FOURIER_WIDTH // HEAD_DIM
IN_COLS = 3 * CONV_WIDTH + POOL_WIDTH + FOURIER_WIDTH
D_FF = ((8 * D_MODEL // 3 + 255) // 256) * 256
ALPHA = (2.0 * DEPTH) ** 0.25
BETA = (8.0 * DEPTH) ** -0.25
LN_EPS = 1e-5
RMS_EPS = 1e-6

kernel_name = "hybrid_conv_pool_fourier_deepnorm_encoder"

def layer_norm(x, g, b):
    xf = x.astype(jnp.float32)
    mu = jnp.mean(xf, axis=-1, keepdims=True)
    var = jnp.mean(jnp.square(xf - mu), axis=-1, keepdims=True)
    return ((xf - mu) * lax.rsqrt(var + LN_EPS)).astype(x.dtype) * g + b

def rms_norm(x, g):
    xf = x.astype(jnp.float32)
    ms = jnp.mean(jnp.square(xf), axis=-1, keepdims=True)
    return (xf * lax.rsqrt(ms + RMS_EPS)).astype(x.dtype) * g

def dwconv3_centred(h, w, b=None):
    hp = jnp.pad(h, ((0, 0), (1, 1), (0, 0)))
    y = hp[:, :-2] * w[0] + hp[:, 1:-1] * w[1] + hp[:, 2:] * w[2]
    return y if b is None else y + b

def multiscale_pool(h):
    bsz, s, c = h.shape
    hf = h.astype(jnp.float32)
    cs = jnp.concatenate([jnp.zeros((bsz, 1, c), jnp.float32), lax.cumsum(hf, axis=1)], axis=1)
    pos = jnp.arange(s)
    outs = []
    for gi, w in enumerate(POOL_WINDOWS):
        half = w // 2
        cg = cs[:, :, gi * POOL_GROUP:(gi + 1) * POOL_GROUP]
        hi = jnp.pad(cg[:, half:], ((0, 0), (0, half), (0, 0)), mode="edge")[:, :s]
        lo = jnp.pad(cg[:, :s - half], ((0, 0), (half, 0), (0, 0)))
        count = (jnp.minimum(pos + half, s) - jnp.maximum(pos - half, 0)).astype(jnp.float32)[None, :, None]
        outs.append((hi - lo) / count)
    pooled = jnp.concatenate(outs, axis=-1)
    return (pooled - hf).astype(h.dtype)

def fourier_mix(h):
    bsz, s, _ = h.shape
    hf = h.astype(jnp.float32).reshape(bsz, s, FOURIER_HEADS, HEAD_DIM)
    f = jnp.fft.fftn(hf, axes=(1, 3), norm="ortho").real
    return f.astype(h.dtype)

def setup_inputs(seed: int = 0) -> dict:
    key = jax.random.key(seed)
    ks = jax.random.split(key, 24)
    f32 = jnp.float32
    nrm = lambda k, shape, scale: jax.random.normal(k, shape, f32) * scale
    gain = lambda k, shape: 1.0 + 0.05 * jax.random.normal(k, shape, f32)
    bias = lambda k, shape: 0.02 * jax.random.normal(k, shape, f32)
    return {
        "x": jax.random.normal(ks[0], (BATCH, SEQ, D_MODEL), f32),
        "ln_in_g": gain(ks[1], (D_MODEL,)),
        "ln_in_b": bias(ks[2], (D_MODEL,)),
        "w_in": nrm(ks[3], (DEPTH, D_MODEL, IN_COLS), D_MODEL ** -0.5),
        "conv_a": nrm(ks[4], (DEPTH, 3, CONV_WIDTH), 3.0 ** -0.5),
        "pool_w": nrm(ks[5], (DEPTH, len(POOL_WINDOWS), POOL_GROUP, POOL_GROUP), POOL_GROUP ** -0.5),
        "pool_scale": gain(ks[6], (DEPTH, POOL_WIDTH)),
        "fourier_w": nrm(ks[7], (DEPTH, FOURIER_HEADS, HEAD_DIM, HEAD_DIM), HEAD_DIM ** -0.5),
        "mix_norm_g": gain(ks[8], (DEPTH, D_MIX)),
        "w_out": nrm(ks[9], (DEPTH, D_MIX, D_MODEL), BETA * D_MIX ** -0.5),
        "ln1_g": gain(ks[10], (DEPTH, D_MODEL)),
        "ln1_b": bias(ks[11], (DEPTH, D_MODEL)),
        "w_gate": nrm(ks[12], (DEPTH, D_MODEL, D_FF), D_MODEL ** -0.5),
        "w_up": nrm(ks[13], (DEPTH, D_MODEL, D_FF), D_MODEL ** -0.5),
        "ffn_conv_w": nrm(ks[14], (DEPTH, 3, D_FF), 3.0 ** -0.5),
        "ffn_conv_b": bias(ks[15], (DEPTH, D_FF)),
        "w_down": nrm(ks[16], (DEPTH, D_FF, D_MODEL), BETA * D_FF ** -0.5),
        "ln2_g": gain(ks[17], (DEPTH, D_MODEL)),
        "ln2_b": bias(ks[18], (DEPTH, D_MODEL)),
    }

def reference(x, ln_in_g, ln_in_b, w_in, conv_a, pool_w, pool_scale, fourier_w, mix_norm_g,
              w_out, ln1_g, ln1_b, w_gate, w_up, ffn_conv_w, ffn_conv_b, w_down, ln2_g, ln2_b):
    bsz, s, _ = x.shape
    x = layer_norm(x, ln_in_g, ln_in_b)
    c0, c1, c2 = CONV_WIDTH, 2 * CONV_WIDTH, 3 * CONV_WIDTH
    c3 = c2 + POOL_WIDTH
    for l in range(DEPTH):
        z = jnp.einsum("bsd,dc->bsc", x, w_in[l])
        gate_b, gate_c, v = z[..., :c0], z[..., c0:c1], z[..., c1:c2]
        y_a = gate_b * dwconv3_centred(gate_c * v, conv_a[l])
        pdiff = multiscale_pool(z[..., c2:c3]).reshape(bsz, s, len(POOL_WINDOWS), POOL_GROUP)
        y_b = jnp.einsum("bsgc,gcd->bsgd", pdiff, pool_w[l]).reshape(bsz, s, POOL_WIDTH) * pool_scale[l]
        fr = fourier_mix(z[..., c3:])
        y_c = jnp.einsum("bshc,hcd->bshd", fr, fourier_w[l]).reshape(bsz, s, FOURIER_WIDTH)
        g = mix_norm_g[l]
        mixed = jnp.concatenate([
            rms_norm(y_a, g[:c0]),
            rms_norm(y_b, g[c0:c0 + POOL_WIDTH]),
            rms_norm(y_c, g[c0 + POOL_WIDTH:]),
        ], axis=-1)
        mix_out = jnp.einsum("bsc,cd->bsd", mixed, w_out[l])
        x = layer_norm(ALPHA * x + mix_out, ln1_g[l], ln1_b[l])
        hg = dwconv3_centred(jnp.einsum("bsd,df->bsf", x, w_gate[l]), ffn_conv_w[l], ffn_conv_b[l])
        hu = jnp.einsum("bsd,df->bsf", x, w_up[l])
        ffn_out = jnp.einsum("bsf,fd->bsd", jax.nn.gelu(hg, approximate=False) * hu, w_down[l])
        x = layer_norm(ALPHA * x + ffn_out, ln2_g[l], ln2_b[l])
    return x


_drawn_inputs = setup_inputs


def setup_inputs(seed=0):
    import zlib

    import numpy as np

    out = dict(_drawn_inputs(seed))
    spreads = {}
    factors = {'pool_scale': 4.291, 'ffn_conv_b': 8.0}
    for name, (base, spread) in spreads.items():
        noise = np.random.default_rng([zlib.crc32(name.encode()), seed]).standard_normal(out[name].shape)
        drawn = base * np.exp(spread * noise) if base else spread * noise
        out[name] = __import__('jax').numpy.asarray(drawn.astype(out[name].dtype))
    for name, factor in factors.items():
        out[name] = (out[name] * factor).astype(out[name].dtype)
    return out
```

```python
import concourse.bass as bass
from concourse import mybir
from contextlib import ExitStack

P = 128
S = 256
TT = S // P
D = 2048
KT = D // P
DEPTH = 2
D_FF = 5632
FT = D_FF // P
ALPHA = (2.0 * DEPTH) ** 0.25
LN_EPS = 1e-5
RMS_EPS = 1e-6
CONV = D // 2
POOLW = D // 4
CONV_TILES = CONV // P
POOL_HALF = (1, 2, 4, 8)
PAD = 8

C_B, C_C, C_V = 0, CONV, 2 * CONV
C_POOL, C_FOUR = 3 * CONV, 3 * CONV + POOLW
MIX_COLS = [C_FOUR, C_POOL, C_C, C_V, C_B, C_C + 512, C_V + 512, C_B + 512]
N_MIX = len(MIX_COLS)
N_PAIR = FT // 4
N_COLG = N_MIX + 2 * N_PAIR

OUT_C = 8 * N_MIX
FFN_C = OUT_C + 2 * KT
DOWN_C = FFN_C + 16 * N_PAIR
LAYER_C = DOWN_C + 2 * FT
RING = 4
AHEAD = 3
LAPS = LAYER_C // RING
PLAPS = LAYER_C // 2 // RING
CREDIT = 2

Q_LNA_G, Q_LNA_B, Q_LN1_G, Q_LN1_B = 0, KT, 2 * KT, 3 * KT
Q_CONV = 4 * KT
Q_PSC = Q_CONV + 3 * CONV_TILES
Q_MIXG = Q_PSC + 4
Q_FCW = Q_MIXG + KT
Q_FCB = Q_FCW + 3 * FT
NPAR = Q_FCB + FT
K_ID, K_ONE5, K_ONE10, K_DFTC, K_INV = 0, P, 2 * P, 3 * P, 5 * P
K_DFTS = K_INV + 4 * S
NCONST = K_DFTS + 4 * S


def build(nc, x, w_in, w_out, w_gate, w_up, w_down, params, small_w, ln_rows, consts, out):
    F32, F32R = mybir.dt.float32, mybir.dt.float32r
    ALU, ACT = mybir.AluOpType, mybir.ActivationFunctionType
    V, A, G, T = nc.vector, nc.scalar, nc.gpsimd, nc.tensor

    with ExitStack() as ctx:
        def sb(name, shape, dt=F32):
            return ctx.enter_context(nc.sbuf_tensor(name, shape, dt))

        def sem(name):
            return ctx.enter_context(nc.semaphore(name))

        resid = sb("resid", [P, TT, D])
        xT = sb("xT", [P, KT, 2 * S], F32R)
        feat = sb("feat", [P, FT, S])
        raw = sb("raw", [P, RING, 2048])
        w_hi = sb("w_hi", [P, RING, 1024], F32R)
        w_lo = sb("w_lo", [P, RING, 1024], F32R)
        m_hi = sb("m_hi", [P, RING, S], F32R)
        m_lo = sb("m_lo", [P, RING, S], F32R)
        scratch = sb("scratch", [P, 8, S])
        xf = scratch[:, :, :].rearrange("p (a k) s -> p a k s", a=2)
        low = scratch[:, 0:4, :]
        mid = scratch[:, 4:8, :]
        padded = sb("padded", [P, 4, S + 2])
        conv = sb("conv", [P, 4, S])
        par = sb("par", [P, NPAR])
        sw = sb("sw", [P, 8, P])
        cst = sb("cst", [P, NCONST])
        neg_half = sb("neg_half", [P, 2 * S])
        stats = sb("stats", [P, TT, 4, 6])
        mv = sb("mv", [P, TT, 2])
        var_eps = sb("var_eps", [P, TT])
        rstd = sb("rstd", [P, TT])
        nmr = sb("nmr", [P, TT])
        ssq = sb("ssq", [P, 3, S])
        ms = sb("ms", [P, 3, S])
        rms = sb("rms", [P, 3, S])
        pin = sb("pin", [P, 1])
        zf = feat[:, 16:20, :]
        uv = feat[:, 20:28, :].rearrange("p (h t) (c) -> p h t c", t=TT)
        sq = feat[:, 20:28, :]
        W = S + 2 * PAD
        flat = feat[:, 28:44, :].rearrange("p a s -> p (a s)")
        ln_g, ln_b = flat[:, 0:D], flat[:, D:2 * D]
        zp = flat[:, 0:4 * W].rearrange("p (a w) -> p a w", a=4)
        win = [flat[:, (1 + i) * 4 * W:(2 + i) * 4 * W].rearrange("p (a w) -> p a w", a=4) for i in range(2)]
        ident = cst[:, K_ID:K_ID + P]
        ones_pool = cst[:, K_ONE5:K_ONE5 + P]
        ones_conv = cst[:, K_ONE10:K_ONE10 + P]
        dft_c = cst[:, K_DFTC:K_DFTC + 2 * P]
        dft_s = cst[:, K_DFTS:K_DFTS + 4 * S].rearrange("p (t s) -> p t s", t=TT)
        inv_count = cst[:, K_INV:K_INV + 4 * S].rearrange("p (a s) -> p a s", a=4)
        ps = ctx.enter_context(nc.psum_tensor("ps", [P, 8, 512], F32))

        panel_landed = [sem(f"panel_landed{i}") for i in range(RING)]
        hi_cut = [sem(f"hi_cut{i}") for i in range(RING)]
        lo_cut = [sem(f"lo_cut{i}") for i in range(RING)]
        used = [sem(f"used{i}") for i in range(RING)]
        slots_seen = sem("slots_seen")
        consts_in, x_in, params_in, ln_rows_in = sem("consts_in"), sem("x_in"), sem("params_in"), sem("ln_rows_in")
        pads_zero, neg_half_set = sem("pads_zero"), sem("neg_half_set")
        y_added, stats_done, mv_done, var_ready = sem("y_added"), sem("stats_done"), sem("mv_done"), sem("var_ready")
        rstd_ready, nmr_ready = sem("rstd_ready"), sem("nmr_ready")
        norm0, norm1 = sem("norm0"), sem("norm1")
        transposed, xf_ready, xT_hi, xT_ready = sem("transposed"), sem("xf_ready"), sem("xT_hi"), sem("xT_ready")
        resid_scaled, resid_ready = sem("resid_scaled"), sem("resid_ready")
        low_copied = sem("low_copied")
        sums_out = sem("sums_out")
        bank_done = sem("bank_done")
        zp_ready, window, pooled = sem("zp_ready"), sem("window"), sem("pooled")
        uv_done, uv_act, uv_dve = sem("uv_done"), sem("uv_act"), sem("uv_dve")
        fr_done, fr_act, fr_dve = sem("fr_done"), sem("fr_act"), sem("fr_dve")
        proj_done, yb_ready, yc_ready = sem("proj_done"), sem("yb_ready"), sem("yc_ready")
        sq_step, ssq_pf = sem("sq_step"), sem("ssq_pf")
        ms_pf_done, ms_pf_ready, rms_pf = sem("ms_pf_done"), sem("ms_pf_ready"), sem("rms_pf")
        cv_ready, mid_ready, tap0 = sem("cv_ready"), sem("mid_ready"), sem("tap0")
        conv_done, ya_ready = sem("conv_done"), sem("ya_ready")
        sqa_step, ssq_a0, sqa1, ssq_a_step = sem("sqa_step"), sem("ssq_a0"), sem("sqa1"), sem("ssq_a_step")
        ms_a_done, ms_a_ready, rms_a = sem("ms_a_done"), sem("ms_a_ready"), sem("rms_a")
        mixed_ready = sem("mixed_ready")
        g_mid, g_tap0, g_conv, gelu_done, h_ready = sem("g_mid"), sem("g_tap0"), sem("g_conv"), sem("gelu_done"), sem("h_ready")
        fin_a, fin_b, stored = sem("fin_a"), sem("fin_b"), sem("stored")
        last_rows_in = sem("last_rows_in")

        block = ctx.enter_context(nc.Block())

        def lap(l, c, i=None, step=0):
            v = LAPS * l + c // RING + 1
            return v if i is None else v + step // RING * i

        def plap(l, c, i=None, step=0):
            v = PLAPS * l + c // 8 + 1
            return v if i is None else v + step // 8 * i

        def bank(s, b):
            return 4 * s + b

        def cut_out(eng, cut, l, chunk, ready):
            k = (chunk - OUT_C) % KT
            if chunk - OUT_C < KT:
                eng.wait_ge(ready, KT * l + k + 1)
            cut(l, chunk, k=k)

        @block.sync
        def _(sp):
            def load(l, p, src, i=None, step=0):
                last_chunk = 2 * (p - RING) + 1
                v = LAPS * l + last_chunk // RING + 1 + CREDIT
                sp.wait_ge(lo_cut[last_chunk % RING], v if i is None else v + 2 * step // RING * i)
                sp.sem_inc(slots_seen, 1)
                a = src.shape[0] // P
                dst = raw[:, p % RING, :].rearrange("p (a n) -> p a n", a=a)
                sp.dma_start(dst, src.rearrange("(a p) n -> p a n", p=P)).then_inc(panel_landed[p % RING], 16)

            with sp.Fori(0, DEPTH) as l:
                wi, wo, wg, wu, wd = (w.rearrange("l k n -> (l k) n") for w in (w_in, w_out, w_gate, w_up, w_down))
                for g, col in enumerate(MIX_COLS):
                    for q in range(4):
                        load(l, 4 * g + q, wi[bass.ds(D * l + 512 * q, 512), col:col + 512])
                for half in range(2):
                    for p in range(KT // 2):
                        row = 2 * P * ((p + 4) % 8)
                        load(l, OUT_C // 2 + 8 * half + p,
                             wo[bass.ds(D * l + row, 2 * P), 1024 * half:1024 * half + 1024])
                with sp.Fori(0, N_PAIR) as i:
                    for u, w in enumerate((wg, wu)):
                        for q in range(4):
                            load(l, FFN_C // 2 + 4 * u + q,
                                 w[bass.ds(D * l + 512 * q, 512), bass.ds(512 * i, 512)], i, 8)
                for half in range(2):
                    first = DOWN_C // 2 + half * FT // 2
                    cols = slice(1024 * half, 1024 * half + 1024)
                    for p in range(2):
                        load(l, first + p, wd[bass.ds(D_FF * l + 2 * P * p, 2 * P), cols])
                    with sp.Fori(0, (FT // 2 - 2) // 4) as i:
                        for p in range(2, 6):
                            load(l, first + p, wd[bass.ds(D_FF * l + 8 * P * i + 2 * P * p, 2 * P), cols], i, 4)
            for n in range(4):
                tt, c = n // 2, (n % 2) * 1024
                sp.wait_ge(fin_b, n + 1)
                sp.dma_start(out[0, tt * P:tt * P + P, c:c + 1024], resid[:, tt, c:c + 1024]).then_inc(stored, 16)
            sp.wait_ge(stored, 64)

        @block.tensor
        def _(pe):
            def wait_chunk(l, c, i=None, step=0):
                pe.wait_ge(lo_cut[c % RING], lap(l, c, i, step) + CREDIT)

            def column_chunk(l, s, c0, c, i=None, step=0):
                wait_chunk(l, c0 + c, i, step)
                slot = c % RING
                for kk in range(2):
                    k = 2 * c + kk
                    for t in range(4):
                        w = slice(512 * kk + P * t, 512 * kk + P * t + P)
                        T.matmul(ps[:, bank(s, t), :], w_hi[:, slot, w], xT[:, k, :], start=(k == 0), stop=False)
                        last = T.matmul(ps[:, bank(s, t), 0:S], w_lo[:, slot, w], xT[:, k, 0:S],
                                        start=False, stop=(k == KT - 1))
                last.then_inc(used[slot], 1)

            def row_chunk(l, s, c, first, final, i=None, step=0):
                wait_chunk(l, c, i, step)
                slot = c % RING
                for cb in range(2):
                    for tt in range(TT):
                        o = ps[:, bank(s, 2 * tt + cb), :]
                        tok, col = slice(P * tt, P * tt + P), slice(512 * cb, 512 * cb + 512)
                        T.matmul(o, m_hi[:, slot, tok], w_hi[:, slot, col], start=first, stop=False)
                        T.matmul(o, m_hi[:, slot, tok], w_lo[:, slot, col], start=False, stop=False)
                        last = T.matmul(o, m_lo[:, slot, tok], w_hi[:, slot, col], start=False, stop=final)
                        if final and (cb, tt) != (1, 1):
                            last.then_inc(bank_done, 1)
                last.then_inc(used[slot], 1)

            def transposes(n, s, q):
                pe.wait_ge(norm0, 4 * n + q + 1)
                pe.wait_ge(norm1, 4 * n + q + 1)
                if q >= 2:
                    pe.wait_ge(xf_ready, 16 * n + 4 * (q - 2) + 4)
                for kk in range(4):
                    for tt in range(TT):
                        o = ps[:, bank(s, 2 * (q % 2) + kk // 2), S * (kk % 2) + P * tt:S * (kk % 2) + P * tt + P]
                        k = 4 * q + kk
                        last = T.transpose(o, resid[:, tt, P * k:P * k + P], ident)
                last.then_inc(transposed, 1)

            def first_column_group(l, n, s, c0):
                transposes(n, 1 - s, 0)
                transposes(n, 1 - s, 1)
                for c in range(8):
                    if c in (2, 4):
                        transposes(n, 1 - s, 1 + c // 2)
                    pe.wait_ge(xT_ready, 8 * n + c + 1)
                    column_chunk(l, s, c0, c)

            pe.wait_ge(consts_in, 16)
            for slot in range(RING):
                pe.sem_inc(used[slot], CREDIT)
            with pe.Fori(0, DEPTH) as l:
                first_column_group(l, 2 * l, 1, 0)
                for g in range(1, N_MIX):
                    s = (g + 1) % 2
                    if g in (5, 6, 7):
                        pe.wait_ge(sums_out, 2 * N_COLG * l + 2 * (g - 2) + 2)
                    if g == 2:
                        pe.wait_ge(uv_act, l + 1)
                        pe.wait_ge(uv_dve, l + 1)
                    if g == 3:
                        pe.wait_ge(fr_act, l + 1)
                        pe.wait_ge(fr_dve, l + 1)
                    if g == 4:
                        pe.wait_ge(yb_ready, l + 1)
                        pe.wait_ge(yc_ready, l + 1)
                    if g == 5:
                        pe.wait_ge(ms_pf_ready, l + 1)
                    for c in range(8):
                        if c == 4 and g == 1:
                            pe.wait_ge(sums_out, 2 * N_COLG * l + 2)
                            for h in range(4):
                                for tt in range(TT):
                                    last = T.matmul(ps[:, 4 + h, S * tt:S * tt + S], zf[:, h, P * tt:P * tt + P],
                                                    dft_c, start=True, stop=True)
                            last.then_inc(uv_done, 1)
                        if c == 4 and g == 2:
                            pe.wait_ge(uv_act, l + 1)
                            pe.wait_ge(uv_dve, l + 1)
                            pe.wait_ge(sums_out, 2 * N_COLG * l + 4)
                            for h in range(4):
                                for n in range(4):
                                    tt, part = n // 2, n % 2
                                    last = T.matmul(ps[:, h // 2, S * (h % 2):S * (h % 2) + S],
                                                    uv[:, h, tt, P * part:P * part + P],
                                                    dft_s[:, tt, S * part:S * part + S], start=(n == 0), stop=(n == 3))
                            last.then_inc(fr_done, 1)
                        if c == 4 and g == 3:
                            pe.wait_ge(fr_act, l + 1)
                            pe.wait_ge(fr_dve, l + 1)
                            pe.wait_ge(pooled, l + 1)
                            pe.wait_ge(params_in, 32 * l + 32)
                            pe.wait_ge(sums_out, 2 * N_COLG * l + 6)
                            for h in range(8):
                                rhs = zf[:, h, :] if h < 4 else zp[:, h - 4, PAD:PAD + S]
                                last = T.matmul(ps[:, 4 + h // 2, S * (h % 2):S * (h % 2) + S], sw[:, h, :], rhs,
                                                start=True, stop=True)
                            last.then_inc(proj_done, 1)
                        if c == 4 and g == 4:
                            pe.wait_ge(ssq_pf, l + 1)
                            pe.wait_ge(sums_out, 2 * N_COLG * l + 8)
                            T.matmul(ps[:, 0, :], ones_pool, ssq[:, 0:2, :].rearrange("p a s -> p (a s)"),
                                     start=True, stop=True).then_inc(ms_pf_done, 1)
                        column_chunk(l, s, 8 * g, c)
                for half in range(2):
                    s, base = 1 - half, OUT_C + KT * half
                    if half == 0:
                        pe.wait_ge(sums_out, 2 * N_COLG * l + 2 * 6 + 2)
                    else:
                        pe.wait_ge(ms_a_ready, l + 1)
                    for c in range(4):
                        row_chunk(l, s, base + c, c == 0, False)
                    if half == 0:
                        pe.wait_ge(ssq_a_step, 3 * l + 3)
                        T.matmul(ps[:, 0, 0:S], ones_conv, ssq[:, 2, :], start=True, stop=True).then_inc(ms_a_done, 1)
                    with pe.Fori(0, KT // 4 - 2) as i:
                        for c in range(4):
                            row_chunk(l, s, base + 4 + c, False, False, i, 4)
                    for c in range(KT - 4, KT):
                        row_chunk(l, s, base + c, False, c == KT - 1)
                first_column_group(l, 2 * l + 1, 0, FFN_C)
                pe.wait_ge(xf_ready, 16 * (2 * l + 1) + 16)
                for c in range(8):
                    column_chunk(l, 1, FFN_C + 8, c)
                with pe.Fori(0, N_PAIR - 1) as i:
                    for u in range(2):
                        pe.wait_ge(sums_out, 2 * N_COLG * l + 2 * (N_MIX + u) + 2 + 4 * i)
                        for c in range(8):
                            column_chunk(l, u, FFN_C + 16 + 8 * u, c, i, 16)
                for half in range(2):
                    base = DOWN_C + FT * half
                    pe.wait_ge(sums_out, 2 * N_COLG * l + 2 * (N_COLG - 2 + half) + 2)
                    for c in range(4):
                        row_chunk(l, half, base + c, c == 0, False)
                    with pe.Fori(0, FT // 4 - 2) as i:
                        for c in range(4):
                            row_chunk(l, half, base + 4 + c, False, False, i, 4)
                    for c in range(FT - 4, FT):
                        row_chunk(l, half, base + c, False, c == FT - 1)

        @block.scalar
        def _(act):
            def cut_hi(l, c, i=None, step=0, k=None):
                slot = c % RING
                act.wait_ge(used[slot], lap(l, c, i, step) - 1 + CREDIT)
                if k is not None:
                    A.activation(m_hi[:, slot, :], feat[:, k, :], ACT.Copy)
                act.wait_ge(panel_landed[c // 2 % RING], 16 * plap(l, c, i, step))
                A.activation(w_hi[:, slot, :], raw[:, c // 2 % RING, 1024 * (c % 2):1024 * (c % 2) + 1024],
                             ACT.Copy).then_inc(hi_cut[slot], 1)

            def copy_low(l, g, st, c_last, i=None, pair=0):
                s = (g + 1) % 2 if g < N_MIX else (g - N_MIX) % 2
                if st == 0:
                    act.wait_ge(used[3], lap(l, c_last, i, 16 if i is not None else 0) + CREDIT)
                A.activation(low[:, 2 * st:2 * st + 2, :], ps[:, bank(s, 2 * st):bank(s, 2 * st) + 2, S:2 * S],
                             ACT.Copy).then_inc(low_copied, 1)

            def centre_tap(tile, w, b, done):
                A.activation(mid[:, tile, :], padded[:, tile, 1:S + 1], ACT.Identity, bias=b, scale=w).then_inc(done, 1)

            def norm_rows(n, q):
                A.activation(resid[:, 1, 512 * q:512 * q + 512], resid[:, 1, 512 * q:512 * q + 512], ACT.Identity,
                             bias=nmr[:, 1:2], scale=rstd[:, 1:2]).then_inc(norm1, 1)

            def read_transposed(n, s, q, qg, qb):
                act.wait_ge(transposed, 4 * n + q + 1)
                if q >= 2:
                    act.wait_ge(xT_ready, 8 * n + 2 * (q - 2) + 2)
                for kk in range(4):
                    k = 4 * q + kk
                    A.activation(xf[:, q % 2, kk, :], ps[:, bank(s, 2 * (q % 2) + kk // 2), S * (kk % 2):S * (kk % 2) + S],
                                 ACT.Identity, bias=par[:, qb + k:qb + k + 1],
                                 scale=par[:, qg + k:qg + k + 1]).then_inc(xf_ready, 1)

            def behind_norm(l, n, s, c0, qg, qb):
                for c in range(AHEAD):
                    cut_hi(l, c0 + c)
                act.wait_ge(nmr_ready, n + 1)
                norm_rows(n, 0)
                norm_rows(n, 1)
                act.wait_ge(params_in, 32 * l + 32)
                read_transposed(n, 1 - s, 0, qg, qb)
                norm_rows(n, 2)
                norm_rows(n, 3)
                read_transposed(n, 1 - s, 1, qg, qb)
                for c in range(8):
                    cut_hi(l, c0 + c + AHEAD)
                    if c in (2, 4):
                        read_transposed(n, 1 - s, 1 + c // 2, qg, qb)

            def gate_hooks(c, l, i, c_last, tile0):
                n_before = 4 * N_PAIR * l + 4 * i if i is not None else 4 * N_PAIR * l + 4 * (N_PAIR - 1)
                g = N_MIX
                if c in (0, 1):
                    copy_low(l, g, c, c_last, i)
                if c in (1, 2):
                    v = 2 * N_COLG * l + 2 * N_MIX
                    v = v + 4 * i if i is not None else v + 4 * (N_PAIR - 1)
                    act.wait_ge(sums_out, v + c)
                    for t in (2 * c - 2, 2 * c - 1):
                        centre_tap(t, par[:, fcol(Q_FCW + FT, tile0, t)], par[:, fcol(Q_FCB, tile0, t)], g_mid)
                if c in (3, 4):
                    for t in (2 * c - 6, 2 * c - 5):
                        act.wait_ge(g_conv, n_before + t + 1)
                        A.activation(feat[:, fcol(0, tile0, t), :], conv[:, t:t + 1, :], ACT.Gelu).then_inc(gelu_done, 1)

            def fcol(base, tile0, t):
                return bass.ds(tile0 + (base + t), 1)

            act.dma_start(cst[:, :], consts).then_inc(consts_in, 16)
            act.dma_start(resid[:, :, :], x[0].rearrange("(a p) n -> p a n", p=P)).then_inc(x_in, 16)

            with act.Fori(0, DEPTH) as l:
                act.dma_start(par[:, :], params[bass.ds(P * l, P), :]).then_inc(params_in, 16)
                act.dma_start(sw[:, :, :].rearrange("p a n -> p (a n)"), small_w[bass.ds(P * l, P), :]).then_inc(params_in, 16)
                act.wait_ge(lo_cut[3], LAPS * l + CREDIT)
                for r, dst in enumerate((ln_g, ln_b)):
                    act.dma_start(dst, ln_rows[bass.ds(2 * (2 * l) + r, 1), :].to_broadcast([P, D])).then_inc(ln_rows_in, 16)
                behind_norm(l, 2 * l, 1, 0, Q_LNA_G, Q_LNA_B)
                for g in range(1, N_MIX + 1):
                    for c in range(8):
                        chunk = 8 * g + c + AHEAD
                        if g == N_MIX:
                            break
                        if chunk >= OUT_C:
                            cut_out(act, cut_hi, l, chunk, mixed_ready)
                        else:
                            cut_hi(l, chunk)
                        if c in (0, 1):
                            copy_low(l, g - 1, c, 8 * g - 1)
                        if g in (4, 7) and c in (2, 3):
                            act.wait_ge(cv_ready, 4 * l + 2 * (g // 6) + c - 1)
                            for t in (2 * c - 4, 2 * c - 3):
                                q = Q_CONV + CONV_TILES + 4 * (g // 6) + t
                                centre_tap(t, par[:, q:q + 1], 0.0, mid_ready)
                        if c == 4 and g == 1:
                            act.wait_ge(uv_done, l + 1)
                            A.activation(uv[:, 0:2, :, :].rearrange("p h t c -> p h (t c)"), ps[:, 4:6, :], ACT.Copy).then_inc(uv_act, 1)
                        if c == 4 and g == 2:
                            act.wait_ge(fr_done, l + 1)
                            A.activation(zf[:, 0:2, :], ps[:, 0, :].rearrange("p (a s) -> p a s", a=2), ACT.Copy).then_inc(fr_act, 1)
                        if c == 4 and g == 3:
                            act.wait_ge(proj_done, l + 1)
                            for t in range(4):
                                last = A.activation(feat[:, t, :], ps[:, 6 + t // 2, S * (t % 2):S * (t % 2) + S], ACT.Copy,
                                                    scale=par[:, Q_PSC + t:Q_PSC + t + 1])
                            last.then_inc(yb_ready, 1)
                        if c == 4 and g == 5:
                            act.wait_ge(resid_ready, 2 * l + 1)
                            for r, dst in enumerate((ln_g, ln_b)):
                                act.dma_start(dst, ln_rows[bass.ds(2 * (2 * l + 1) + r, 1), :].to_broadcast([P, D])).then_inc(ln_rows_in, 16)
                for c in range(2 * KT):
                    if c + AHEAD < 2 * KT:
                        cut_out(act, cut_hi, l, OUT_C + c + AHEAD, mixed_ready)
                    if c in (0, 1):
                        copy_low(l, N_MIX - 1, c, OUT_C - 1)
                    if c == 2:
                        act.wait_ge(ya_ready, 4 * l + 4)
                        act.wait_ge(ssq_a0, l + 1)
                        A.activation(sq[:, 0:4, :], feat[:, 12:16, :], ACT.Square).then_inc(sqa1, 1)
                behind_norm(l, 2 * l + 1, 0, FFN_C, Q_LN1_G, Q_LN1_B)
                act.wait_ge(resid_ready, 2 * l + 2)
                with act.Fori(0, N_PAIR - 1) as i:
                    for c in range(8):
                        cut_hi(l, FFN_C + 8 + c + AHEAD, i, 16)
                        gate_hooks(c, l, i, FFN_C + 7, 4 * i)
                    for c in range(8):
                        cut_hi(l, FFN_C + 16 + c + AHEAD, i, 16)
                        if c in (0, 1):
                            copy_low(l, N_MIX + 1, c, FFN_C + 15, i)
                for c in range(8):
                    chunk = DOWN_C - 8 + c + AHEAD
                    if chunk >= DOWN_C:
                        cut_hi(l, chunk, k=chunk - DOWN_C)
                    else:
                        cut_hi(l, chunk)
                    gate_hooks(c, l, None, DOWN_C - 9, 4 * (N_PAIR - 1))
                for half in range(2):
                    base = DOWN_C + FT * half
                    for c in range(8):
                        if half == 0 and c == 2:
                            act.wait_ge(h_ready, 2 * N_PAIR * l + 2 * N_PAIR)
                        cut_hi(l, base + c + AHEAD, k=c + AHEAD)
                        if half == 0 and c in (0, 1):
                            copy_low(l, N_COLG - 1, c, DOWN_C - 1)
                    with act.Fori(0, FT // 8 - 1) as i:
                        for c in range(8):
                            cut_hi(l, base + 8 + c + AHEAD, i, 8, k=bass.ds(8 * i + (8 + c + AHEAD), 1))
                    for c in range(FT - 4, FT):
                        if c + AHEAD < FT or half == 0:
                            cut_hi(l, base + c + AHEAD, k=(c + AHEAD) % FT)

        @block.vector
        def _(dve):
            def cut_lo(l, c, i=None, step=0, k=None):
                slot = c % RING
                dve.wait_ge(hi_cut[slot], lap(l, c, i, step))
                if k is not None:
                    V.tensor_tensor(m_lo[:, slot, :], feat[:, k, :], m_hi[:, slot, :].bitcast(F32), ALU.subtract)
                V.tensor_tensor(w_lo[:, slot, :], raw[:, c // 2 % RING, 1024 * (c % 2):1024 * (c % 2) + 1024],
                                w_hi[:, slot, :].bitcast(F32), ALU.subtract).then_inc(lo_cut[slot], 1)

            def add_halves(l, g, st, dst, i=None):
                s = (g + 1) % 2 if g < N_MIX else (g - N_MIX) % 2
                v = 2 * N_COLG * l + 2 * g + st + 1
                dve.wait_ge(low_copied, v if i is None else v + 4 * i)
                V.tensor_tensor(dst, ps[:, bank(s, 2 * st):bank(s, 2 * st) + 2, 0:S], low[:, 2 * st:2 * st + 2, :],
                                ALU.add).then_inc(sums_out, 1)

            def after_sum(l, g, st, i=None):
                v = 2 * N_COLG * l + 2 * g + st + 1
                dve.wait_ge(sums_out, v if i is None else v + 4 * i)

            def add_residual(l, n, s, j):
                cb, tt = j // 2, j % 2
                if j < 3:
                    dve.wait_ge(bank_done, 12 * l + 3 * n + j + 1)
                else:
                    last_chunk = (OUT_C + KT * (n + 1) if n < 2 else DOWN_C + FT * (n - 1)) - 1
                    dve.wait_ge(used[3], lap(l, last_chunk) + CREDIT)
                col = 1024 * (n % 2) + 512 * cb
                y = resid[:, tt, col:col + 512]
                V.scalar_tensor_tensor(out=y, in0=y, scalar=ALPHA, in1=ps[:, bank(s, 2 * tt + cb), :],
                                       op0=ALU.mult, op1=ALU.add).then_inc(y_added, 1)
                dve.wait_ge(y_added, 16 * l + 4 * n + j + 1)
                V.bn_stats(stats[:, tt, 2 * (n % 2) + cb, :], y).then_inc(stats_done, 1)

            def mean_var(n):
                dve.wait_ge(stats_done, 8 * n + 8)
                V.memset(pin[:, :], 0.0)
                for tt in range(TT):
                    last = V.bn_aggr(mv[:, tt, :], stats[:, tt, :, :].rearrange("p a b -> p (a b)"))
                last.then_inc(mv_done, 1)
                dve.wait_ge(mv_done, n + 1)
                V.tensor_scalar(var_eps[:, :], mv[:, :, 1], LN_EPS, None, ALU.add).then_inc(var_ready, 1)

            def cut_x(n, p):
                q, kk = p // 2, 2 * (p % 2)
                src = xf[:, q % 2, kk:kk + 2, :]
                dve.wait_ge(xf_ready, 16 * n + 2 * p + 2)
                V.tensor_copy(xT[:, 2 * p:2 * p + 2, 0:S], src).then_inc(xT_hi, 1)
                dve.wait_ge(xT_hi, 8 * n + p + 1)
                V.tensor_tensor(xT[:, 2 * p:2 * p + 2, S:2 * S], src, xT[:, 2 * p:2 * p + 2, 0:S].bitcast(F32),
                                ALU.subtract).then_inc(xT_ready, 1)

            def behind_norm(l, n, c0):
                mean_var(n)
                cut_lo(l, c0)
                dve.wait_ge(rstd_ready, n + 1)
                V.scalar_tensor_tensor(out=nmr[:, :], in0=mv[:, :, 0], scalar=-1.0, in1=rstd[:, :],
                                       op0=ALU.mult, op1=ALU.mult).then_inc(nmr_ready, 1)
                for q in range(4):
                    y = resid[:, 0, 512 * q:512 * q + 512]
                    V.tensor_scalar(y, y, mv[:, 0, 0:1], rstd[:, 0:1], ALU.subtract, ALU.mult).then_inc(norm0, 1)
                cut_x(n, 0)
                cut_x(n, 1)
                cut_lo(l, c0 + 1)
                cut_x(n, 2)
                cut_x(n, 3)
                cut_lo(l, c0 + 2)
                for c in range(8):
                    cut_lo(l, c0 + c + AHEAD)
                    if c in (2, 4):
                        cut_x(n, 2 + c)
                        cut_x(n, 3 + c)

            def outer_taps(t, w0, w2, mid_sem, n_mid, tap_sem, n_tap, done):
                for u in (t, t + 1):
                    dve.wait_ge(mid_sem, n_mid + u + 1)
                    V.scalar_tensor_tensor(out=conv[:, u, :], in0=padded[:, u, 0:S], scalar=w0(u), in1=mid[:, u, :],
                                           op0=ALU.mult, op1=ALU.add).then_inc(tap_sem, 1)
                for u in (t, t + 1):
                    dve.wait_ge(tap_sem, n_tap + u + 1)
                    V.scalar_tensor_tensor(out=conv[:, u, :], in0=padded[:, u, 2:S + 2], scalar=w2(u), in1=conv[:, u, :],
                                           op0=ALU.mult, op1=ALU.add).then_inc(done, 1)

            def gate_hooks(c, l, i, g, tile0):
                if c in (0, 1):
                    add_halves(l, g, c, padded[:, 2 * c:2 * c + 2, 1:S + 1], i)
                if c in (2, 3):
                    n = 4 * N_PAIR * l + (4 * i if i is not None else 4 * (N_PAIR - 1))
                    outer_taps(2 * c - 4, lambda u: par[:, bass.ds(tile0 + (Q_FCW + u), 1)],
                               lambda u: par[:, bass.ds(tile0 + (Q_FCW + 2 * FT + u), 1)], g_mid, n, g_tap0, n, g_conv)

            def up_hooks(c, l, i, g, tile0):
                if c in (0, 1):
                    add_halves(l, g, c, conv[:, 2 * c:2 * c + 2, :], i)
                    after_sum(l, g, c, i)
                    h = feat[:, bass.ds(tile0 + 2 * c, 2), :]
                    V.tensor_tensor(h, h, conv[:, 2 * c:2 * c + 2, :], ALU.mult).then_inc(h_ready, 1)

            def scale_mixed(l, k, r):
                V.scalar_tensor_tensor(out=feat[:, k, :], in0=feat[:, k, :], scalar=par[:, Q_MIXG + k:Q_MIXG + k + 1],
                                       in1=rms[:, r, :], op0=ALU.mult, op1=ALU.mult).then_inc(mixed_ready, 1)

            def conv_output(l, grp, g, st):
                t = 8 + 4 * grp + 2 * st
                add_halves(l, g, st, feat[:, t:t + 2, :])
                after_sum(l, g, st)
                V.tensor_tensor(feat[:, t:t + 2, :], feat[:, t:t + 2, :], conv[:, 2 * st:2 * st + 2, :],
                                ALU.mult).then_inc(ya_ready, 1)

            for slot in range(RING):
                dve.sem_inc(lo_cut[slot], CREDIT)
            V.memset(neg_half[:, :], -0.5).then_inc(neg_half_set, 1)
            V.memset(padded[:, :, :], 0.0).then_inc(pads_zero, 1)
            dve.wait_ge(x_in, 16)
            for tt in range(TT):
                for q in range(4):
                    V.bn_stats(stats[:, tt, q, :], resid[:, tt, 512 * q:512 * q + 512]).then_inc(stats_done, 1)
            dve.wait_ge(consts_in, 16)
            dve.wait_ge(pads_zero, 1)
            with dve.Fori(0, DEPTH) as l:
                behind_norm(l, 2 * l, 0)
                dve.wait_ge(params_in, 32 * l + 32)
                for g in range(1, N_MIX):
                    for c in range(8):
                        chunk = 8 * g + c + AHEAD
                        if chunk >= OUT_C:
                            cut_out(dve, cut_lo, l, chunk, mixed_ready)
                        else:
                            cut_lo(l, chunk)
                        two = slice(2 * c, 2 * c + 2)
                        if c in (0, 1):
                            if g == 1:
                                add_halves(l, 0, c, zf[:, two, :])
                            if g == 2:
                                if c == 0:
                                    dve.wait_ge(resid_ready, 2 * l + 1)
                                    V.memset(zp[:, :, 0:PAD], 0.0)
                                    V.memset(zp[:, :, PAD + S:W], 0.0)
                                add_halves(l, 1, c, zp[:, two, PAD:PAD + S])
                            if g in (3, 6):
                                add_halves(l, g - 1, c, conv[:, two, :])
                            if g in (4, 7):
                                add_halves(l, g - 1, c, padded[:, two, 1:S + 1])
                                after_sum(l, g - 1, c)
                                V.tensor_tensor(padded[:, two, 1:S + 1], padded[:, two, 1:S + 1], conv[:, two, :],
                                                ALU.mult).then_inc(cv_ready, 1)
                            if g == 5:
                                conv_output(l, 0, 4, c)
                        if g in (4, 7) and c in (3, 4):
                            grp = g // 6
                            q = Q_CONV + 4 * grp
                            n = 8 * l + 4 * grp
                            outer_taps(2 * c - 6, lambda u: par[:, q + u:q + u + 1],
                                       lambda u: par[:, q + 2 * CONV_TILES + u:q + 2 * CONV_TILES + u + 1],
                                       mid_ready, n, tap0, n, conv_done)
                        if c == 4 and g == 1:
                            dve.wait_ge(uv_done, l + 1)
                            V.tensor_copy(uv[:, 2:4, :, :].rearrange("p h t c -> p h (t c)"), ps[:, 6:8, :]).then_inc(uv_dve, 1)
                        if c == 4 and g == 2:
                            dve.wait_ge(fr_done, l + 1)
                            V.tensor_copy(zf[:, 2:4, :], ps[:, 1, :].rearrange("p (a s) -> p a s", a=2)).then_inc(fr_dve, 1)
                        if c == 4 and g == 3:
                            dve.wait_ge(proj_done, l + 1)
                            V.tensor_copy(feat[:, 4:8, :], ps[:, 4:6, :].rearrange("p b (a s) -> p (b a) s", a=2)).then_inc(yc_ready, 1)
                        if c == 5 and g == 4:
                            dve.wait_ge(ms_pf_done, l + 1)
                            V.tensor_scalar(ms[:, 0:2, :], ps[:, 0, :].rearrange("p (a s) -> p a s", a=2), RMS_EPS, None,
                                            ALU.add).then_inc(ms_pf_ready, 1)
                        if g == 6 and c in (4, 5):
                            if c == 4:
                                dve.wait_ge(rms_pf, l + 1)
                            for k in range(4 * c - 16, 4 * c - 12):
                                scale_mixed(l, k, c - 4)
                for c in range(2 * KT):
                    if c + AHEAD < 2 * KT:
                        cut_out(dve, cut_lo, l, OUT_C + c + AHEAD, mixed_ready)
                    if c in (0, 1):
                        conv_output(l, 1, N_MIX - 1, c)
                    if c == 2:
                        dve.wait_ge(sqa1, l + 1)
                        V.tensor_tensor(sq[:, 0:2, :], sq[:, 0:2, :], sq[:, 2:4, :], ALU.add).then_inc(ssq_a_step, 1)
                        dve.wait_ge(ssq_a_step, 3 * l + 1)
                        V.tensor_tensor(sq[:, 0, :], sq[:, 0, :], sq[:, 1, :], ALU.add).then_inc(ssq_a_step, 1)
                        dve.wait_ge(ssq_a_step, 3 * l + 2)
                        dve.wait_ge(ssq_a0, l + 1)
                        V.tensor_tensor(ssq[:, 2, :], ssq[:, 2, :], sq[:, 0, :], ALU.add).then_inc(ssq_a_step, 1)
                    if c == 4:
                        dve.wait_ge(ms_a_done, l + 1)
                        V.tensor_scalar(ms[:, 2, :], ps[:, 0, 0:S], RMS_EPS, None, ALU.add).then_inc(ms_a_ready, 1)
                        dve.wait_ge(rms_a, l + 1)
                    if c in (4, 5):
                        for k in range(8 + 4 * (c - 4), 12 + 4 * (c - 4)):
                            scale_mixed(l, k, 2)
                    if c in (KT, KT + 1):
                        for j in (2 * (c - KT), 2 * (c - KT) + 1):
                            add_residual(l, 0, 1, j)
                for j in range(4):
                    add_residual(l, 1, 0, j)
                behind_norm(l, 2 * l + 1, FFN_C)
                with dve.Fori(0, N_PAIR - 1) as i:
                    for c in range(8):
                        cut_lo(l, FFN_C + 8 + c + AHEAD, i, 16)
                        gate_hooks(c, l, i, N_MIX, 4 * i)
                    for c in range(8):
                        cut_lo(l, FFN_C + 16 + c + AHEAD, i, 16)
                        up_hooks(c, l, i, N_MIX + 1, 4 * i)
                for c in range(8):
                    chunk = DOWN_C - 8 + c + AHEAD
                    if chunk >= DOWN_C:
                        if chunk == DOWN_C:
                            dve.wait_ge(h_ready, 2 * N_PAIR * l + 2 * N_PAIR - 2)
                        cut_lo(l, chunk, k=chunk - DOWN_C)
                    else:
                        cut_lo(l, chunk)
                    gate_hooks(c, l, None, N_COLG - 2, 4 * (N_PAIR - 1))
                for half in range(2):
                    base = DOWN_C + FT * half
                    for c in range(8):
                        if half == 0 and c == 2:
                            dve.wait_ge(h_ready, 2 * N_PAIR * l + 2 * N_PAIR)
                        cut_lo(l, base + c + AHEAD, k=c + AHEAD)
                        if half == 0:
                            up_hooks(c, l, None, N_COLG - 1, 4 * (N_PAIR - 1))
                        elif c in (0, 1):
                            for j in (2 * c, 2 * c + 1):
                                add_residual(l, 2, 0, j)
                    with dve.Fori(0, FT // 8 - 1) as i:
                        for c in range(8):
                            cut_lo(l, base + 8 + c + AHEAD, i, 8, k=bass.ds(8 * i + (8 + c + AHEAD), 1))
                    for c in range(FT - 4, FT):
                        if c + AHEAD < FT or half == 0:
                            cut_lo(l, base + c + AHEAD, k=(c + AHEAD) % FT)
                for j in range(4):
                    add_residual(l, 3, 1, j)
            n = 2 * DEPTH
            mean_var(n)
            dve.wait_ge(rstd_ready, n + 1)
            dve.wait_ge(last_rows_in, 32)
            for j in range(4):
                tt, c = j // 2, (j % 2) * 1024
                y = resid[:, tt, c:c + 1024]
                V.scalar_tensor_tensor(out=y, in0=y, scalar=mv[:, tt, 0:1], in1=ln_g[:, c:c + 1024],
                                       op0=ALU.subtract, op1=ALU.mult).then_inc(fin_a, 1)
                dve.wait_ge(fin_a, j + 1)
                V.scalar_tensor_tensor(out=y, in0=y, scalar=rstd[:, tt:tt + 1], in1=ln_b[:, c:c + 1024],
                                       op0=ALU.mult, op1=ALU.add).then_inc(fin_b, 1)

        @block.gpsimd
        def _(pool):
            def power(src, dst, width, ready, n, done):
                pool.wait_ge(ready, n)
                G.tensor_tensor(dst, src, neg_half[:, 0:width], ALU.pow).then_inc(done, 1)

            def make_residual(n):
                pool.wait_ge(ln_rows_in, 32 * n + 32)
                pool.wait_ge(transposed, 4 * n + 4)
                for tt in range(TT):
                    G.tensor_tensor(resid[:, tt, :], resid[:, tt, :], ln_g, ALU.mult).then_inc(resid_scaled, 1)
                for tt in range(TT):
                    pool.wait_ge(resid_scaled, 2 * n + tt + 1)
                    last = G.tensor_tensor(resid[:, tt, :], resid[:, tt, :], ln_b, ALU.add)
                last.then_inc(resid_ready, 1)

            pool.wait_ge(neg_half_set, 1)
            pool.wait_ge(consts_in, 16)
            with pool.Fori(0, DEPTH) as l:
                power(var_eps[:, :], rstd[:, :], TT, var_ready, 2 * l + 1, rstd_ready)
                make_residual(2 * l)
                pool.wait_ge(sums_out, 2 * N_COLG * l + 4)
                src, lo_edge, hi_edge = zp, 0, W
                for lev, half in enumerate(POOL_HALF):
                    sh = max(half // 2, 0)
                    dst = win[lev % 2]
                    if lev == 0:
                        lo_edge = 1
                        a, b = zp[:, :, 0:W - 1], zp[:, :, 1:W]
                        o = dst[:, :, 1:W]
                    else:
                        lo_edge, hi_edge = lo_edge + sh, hi_edge - sh
                        a = src[:, lev:4, lo_edge - sh:hi_edge - sh]
                        b = src[:, lev:4, lo_edge + sh:hi_edge + sh]
                        o = dst[:, lev:4, lo_edge:hi_edge]
                        pool.wait_ge(window, 9 * l + lev)
                    G.tensor_tensor(o, a, b, ALU.add).then_inc(window, 1)
                    src = dst
                pool.wait_ge(window, 9 * l + 4)
                for g in range(4):
                    o = win[g % 2][:, g, PAD:PAD + S]
                    G.tensor_tensor(o, o, inv_count[:, g, :], ALU.mult).then_inc(window, 1)
                for g in range(4):
                    pool.wait_ge(window, 9 * l + 5 + g)
                    last = G.tensor_tensor(zp[:, g, PAD:PAD + S], win[g % 2][:, g, PAD:PAD + S], zp[:, g, PAD:PAD + S],
                                           ALU.subtract)
                    if g == 0:
                        last.then_inc(window, 1)
                last.then_inc(pooled, 1)
                pool.wait_ge(yb_ready, l + 1)
                pool.wait_ge(yc_ready, l + 1)
                G.tensor_tensor(sq[:, :, :], feat[:, 0:8, :], feat[:, 0:8, :], ALU.mult).then_inc(sq_step, 1)
                sqv = sq.rearrange("p (g t) s -> p g t s", g=2)
                pool.wait_ge(sq_step, 2 * l + 1)
                G.tensor_tensor(sqv[:, :, 0:2, :], sqv[:, :, 0:2, :], sqv[:, :, 2:4, :], ALU.add).then_inc(sq_step, 1)
                pool.wait_ge(sq_step, 2 * l + 2)
                G.tensor_tensor(ssq[:, 0:2, :], sqv[:, :, 0, :], sqv[:, :, 1, :], ALU.add).then_inc(ssq_pf, 1)
                power(ms[:, 0:2, :].rearrange("p a s -> p (a s)"), rms[:, 0:2, :].rearrange("p a s -> p (a s)"), 2 * S,
                      ms_pf_ready, l + 1, rms_pf)
                pool.wait_ge(ya_ready, 4 * l + 2)
                pool.wait_ge(ssq_pf, l + 1)
                G.tensor_tensor(sq[:, 0:4, :], feat[:, 8:12, :], feat[:, 8:12, :], ALU.mult).then_inc(sqa_step, 1)
                pool.wait_ge(sqa_step, 2 * l + 1)
                G.tensor_tensor(sq[:, 0:2, :], sq[:, 0:2, :], sq[:, 2:4, :], ALU.add).then_inc(sqa_step, 1)
                pool.wait_ge(sqa_step, 2 * l + 2)
                G.tensor_tensor(ssq[:, 2, :], sq[:, 0, :], sq[:, 1, :], ALU.add).then_inc(ssq_a0, 1)
                power(ms[:, 2, :], rms[:, 2, :], S, ms_a_ready, l + 1, rms_a)
                power(var_eps[:, :], rstd[:, :], TT, var_ready, 2 * l + 2, rstd_ready)
                make_residual(2 * l + 1)
            n = 2 * DEPTH
            pool.wait_ge(lo_cut[3], LAPS * DEPTH + CREDIT)
            for r, dst in enumerate((ln_g, ln_b)):
                pool.dma_start(dst, ln_rows[2 * n + r:2 * n + r + 1, :].to_broadcast([P, D])).then_inc(last_rows_in, 16)
            power(var_eps[:, :], rstd[:, :], TT, var_ready, n + 1, rstd_ready)


def kernel(**inputs):
    import numpy as np
    import concourse.bacc as bacc
    from concourse import mybir
    from concourse.bass_utils import run_bass_kernel_spmd as run

    f = np.float32
    a = {k: np.ascontiguousarray(v) for k, v in inputs.items()}

    def chan(v):
        return v.reshape(-1, v.shape[-1] // P, P).transpose(2, 0, 1).reshape(P, -1)

    def used_order(v):
        return np.concatenate([v[CONV:], v[:CONV]])

    ln_g = [a["ln_in_g"]] + [a[f"ln{j}_g"][l] for l in range(DEPTH) for j in (1, 2)]
    ln_b = [a["ln_in_b"]] + [a[f"ln{j}_b"][l] for l in range(DEPTH) for j in (1, 2)]
    params = np.concatenate([np.concatenate([
        chan(ln_g[2 * l]), chan(ln_b[2 * l]), chan(ln_g[2 * l + 1]), chan(ln_b[2 * l + 1]), chan(a["conv_a"][l]),
        chan(a["pool_scale"][l]), chan(used_order(a["mix_norm_g"][l])), chan(a["ffn_conv_w"][l]),
        chan(a["ffn_conv_b"][l])], axis=1) for l in range(DEPTH)])
    small_w = np.concatenate([np.concatenate([a["fourier_w"][l], a["pool_w"][l]]).transpose(1, 0, 2).reshape(P, -1)
                              for l in range(DEPTH)])
    ln_rows = np.stack([v for g, b in zip(ln_g, ln_b) for v in (g, b)])

    c, t = np.arange(P), np.arange(S)
    ang_c = 2 * np.pi * (np.outer(c, c) % P) / P
    ang_t = 2 * np.pi * (np.outer(t, t) % S) / S
    dft_c = np.concatenate([np.cos(ang_c), np.sin(ang_c)], axis=1) / np.sqrt(P)
    dft_t = np.concatenate([np.cos(ang_t), -np.sin(ang_t)], axis=1) / np.sqrt(S)
    inv = np.stack([1.0 / (np.minimum(t + h, S) - np.maximum(t - h, 0)) for h in POOL_HALF]).reshape(1, -1)
    consts = np.concatenate([np.eye(P), np.full((P, P), 1 / POOLW), np.full((P, P), 1 / CONV), dft_c,
                             np.broadcast_to(inv, (P, 4 * S)), dft_t[:P], dft_t[P:]], axis=1).astype(f)

    arrays = {"x": a["x"], "w_in": a["w_in"], "w_out": a["w_out"], "w_gate": a["w_gate"], "w_up": a["w_up"],
              "w_down": a["w_down"], "params": params, "small_w": small_w, "ln_rows": ln_rows, "consts": consts}
    nc = bacc.Bacc("TRN2", target_bir_lowering=False, num_devices=1)
    arrays = {k: np.ascontiguousarray(v) for k, v in arrays.items()}
    args = [nc.dram_tensor(k, v.shape, mybir.dt.from_np(v.dtype), kind="ExternalInput").ap() for k, v in arrays.items()]
    out = nc.dram_tensor("out", (1, S, D), mybir.dt.float32, kind="ExternalOutput").ap()
    build(nc, *args, out)
    return run(nc, [arrays], core_ids=[0]).results[0]["out"]
```

```python
import concourse.bass as bass
from concourse import mybir
from contextlib import ExitStack

P = 128
S = 256
TT = S // P
D = 2048
KT = D // P
DEPTH = 2
D_FF = 5632
FT = D_FF // P
ALPHA = (2.0 * DEPTH) ** 0.25
LN_EPS = 1e-5
RMS_EPS = 1e-6
CONV = D // 2
POOLW = D // 4
CONV_TILES = CONV // P
POOL_HALF = (1, 2, 4, 8)
PAD = 8

C_B, C_C, C_V = 0, CONV, 2 * CONV
C_POOL, C_FOUR = 3 * CONV, 3 * CONV + POOLW
MIX_COLS = [C_FOUR, C_POOL, C_C, C_V, C_B, C_C + 512, C_V + 512, C_B + 512]
N_MIX = len(MIX_COLS)
N_PAIR = FT // 4
N_COLG = N_MIX + 2 * N_PAIR

OUT_C = 8 * N_MIX
OUT_PARTS = [(0, 4, 0), (4, 4, 1), (8, 8, 2)]
FFN_C = OUT_C + 2 * KT
DOWN_C = FFN_C + 16 * N_PAIR
LAYER_C = DOWN_C + 2 * FT
RING = 4
AHEAD = 3
LAPS = LAYER_C // RING
PLAPS = LAYER_C // 2 // RING
CREDIT = 2

Q_LNA_G, Q_LNA_B, Q_LN1_G, Q_LN1_B = 0, KT, 2 * KT, 3 * KT
Q_CONV = 4 * KT
Q_PSC = Q_CONV + 3 * CONV_TILES
Q_MIXG = Q_PSC + 4
Q_FCW = Q_MIXG + KT
Q_FCB = Q_FCW + 3 * FT
NPAR = Q_FCB + FT
K_ID, K_ONE5, K_ONE10, K_DFTC = 0, P, P + 1, P + 2
K_INV = K_DFTC + 2 * P
K_DFTS = K_INV + 4 * S
NCONST = K_DFTS + 4 * S


def build(nc, x, w_in, w_out, w_gate, w_up, w_down, params, small_w, ln_rows, consts, out):
    F32, F32R = mybir.dt.float32, mybir.dt.float32r
    ALU, ACT = mybir.AluOpType, mybir.ActivationFunctionType
    V, A, G, T = nc.vector, nc.scalar, nc.gpsimd, nc.tensor

    with ExitStack() as ctx:
        def sb(name, shape, dt=F32):
            return ctx.enter_context(nc.sbuf_tensor(name, shape, dt))

        def sem(name):
            return ctx.enter_context(nc.semaphore(name))

        resid = sb("resid", [P, TT, D])
        xT = sb("xT", [P, KT, 2 * S], F32R)
        feat = sb("feat", [P, FT, S])
        raw = sb("raw", [P, RING, 2048])
        w_hi = sb("w_hi", [P, RING, 1024], F32R)
        w_lo = sb("w_lo", [P, RING, 1024], F32R)
        m_hi = sb("m_hi", [P, RING, S], F32R)
        m_lo = sb("m_lo", [P, RING, S], F32R)
        scratch = sb("scratch", [P, 8, S])
        xf = scratch[:, :, :].rearrange("p (a k) s -> p a k s", a=2)
        low = scratch[:, 0:4, :]
        mid = scratch[:, 4:8, :]
        padded = sb("padded", [P, 4, S + 2])
        conv = sb("conv", [P, 4, S])
        par = sb("par", [P, NPAR])
        sw = sb("sw", [P, 8, P])
        cst = sb("cst", [P, NCONST])
        neg_half = sb("neg_half", [P, 2 * TT])
        stats = sb("stats", [P, TT, 4, 6])
        mv = sb("mv", [P, TT, 2])
        var_eps = sb("var_eps", [P, TT])
        rstd = sb("rstd", [P, TT])
        nmr = sb("nmr", [P, TT])
        ssq = sb("ssq", [P, 3, S])
        ms = sb("ms", [P, 3, TT])
        rms = sb("rms", [P, 3, TT])
        norm_eps = sb("norm_eps", [P, 1])
        pin = sb("pin", [P, 1])
        zf = feat[:, 16:20, :]
        uv = feat[:, 20:28, :].rearrange("p (h t) (c) -> p h t c", t=TT)
        sq = feat[:, 20:28, :]
        W = S + 2 * PAD
        flat = feat[:, 28:44, :].rearrange("p a s -> p (a s)")
        ln_g, ln_b = flat[:, 0:D], flat[:, D:2 * D]
        zp = flat[:, 0:4 * W].rearrange("p (a w) -> p a w", a=4)
        win = [flat[:, (1 + i) * 4 * W:(2 + i) * 4 * W].rearrange("p (a w) -> p a w", a=4) for i in range(2)]
        ident = cst[:, K_ID:K_ID + P]
        ones_pool = cst[:, K_ONE5:K_ONE5 + 1]
        ones_conv = cst[:, K_ONE10:K_ONE10 + 1]
        dft_c = cst[:, K_DFTC:K_DFTC + 2 * P]
        dft_s = cst[:, K_DFTS:K_DFTS + 4 * S].rearrange("p (t s) -> p t s", t=TT)
        inv_count = cst[:, K_INV:K_INV + 4 * S].rearrange("p (a s) -> p a s", a=4)
        ps = ctx.enter_context(nc.psum_tensor("ps", [P, 8, 512], F32))

        panel_landed = [sem(f"panel_landed{i}") for i in range(RING)]
        hi_cut = [sem(f"hi_cut{i}") for i in range(RING)]
        lo_cut = [sem(f"lo_cut{i}") for i in range(RING)]
        used = [sem(f"used{i}") for i in range(RING)]
        slots_seen = sem("slots_seen")
        tables_in = sem("tables_in")
        consts_in, params_in, ln_rows_in = sem("consts_in"), sem("params_in"), sem("ln_rows_in")
        small_w_in = sem("small_w_in")
        x_in = [sem(f"x_in{tt}") for tt in range(TT)]
        eps_set = sem("eps_set")
        pads_zero, neg_half_set = sem("pads_zero"), sem("neg_half_set")
        y_added, stats_done, mv_done, var_ready = sem("y_added"), sem("stats_done"), sem("mv_done"), sem("var_ready")
        rstd_ready, nmr_ready = sem("rstd_ready"), sem("nmr_ready")
        norm0, norm1 = sem("norm0"), sem("norm1")
        transposed, xf_ready, xT_hi, xT_ready = sem("transposed"), sem("xf_ready"), sem("xT_hi"), sem("xT_ready")
        resid_scaled, resid_ready = sem("resid_scaled"), sem("resid_ready")
        low_copied = sem("low_copied")
        sums_out = sem("sums_out")
        bank_done = sem("bank_done")
        zp_ready, window, pooled = sem("zp_ready"), sem("window"), sem("pooled")
        uv_done, uv_act, uv_dve = sem("uv_done"), sem("uv_act"), sem("uv_dve")
        fr_done, fr_act, fr_dve = sem("fr_done"), sem("fr_act"), sem("fr_dve")
        proj_done, yb_ready, yc_ready = sem("proj_done"), sem("yb_ready"), sem("yc_ready")
        sq_step, ssq_pf = sem("sq_step"), sem("ssq_pf")
        ms_pf_done, ms_pf_ready, rms_pf = sem("ms_pf_done"), sem("ms_pf_ready"), sem("rms_pf")
        cv_ready, mid_ready, tap0 = sem("cv_ready"), sem("mid_ready"), sem("tap0")
        conv_done, ya_ready = sem("conv_done"), sem("ya_ready")
        sqa_step, ssq_a = sem("sqa_step"), sem("ssq_a")
        ms_a_done, ms_a_ready, rms_a = sem("ms_a_done"), sem("ms_a_ready"), sem("rms_a")
        g_mid, g_tap0, g_conv, gelu_done, h_ready = sem("g_mid"), sem("g_tap0"), sem("g_conv"), sem("gelu_done"), sem("h_ready")
        fin_a, fin_b, stored = sem("fin_a"), sem("fin_b"), sem("stored")
        last_rows_in = sem("last_rows_in")

        block = ctx.enter_context(nc.Block())

        def lap(l, c, i=None, step=0):
            v = LAPS * l + c // RING + 1
            return v if i is None else v + step // RING * i

        def plap(l, c, i=None, step=0):
            v = PLAPS * l + c // 8 + 1
            return v if i is None else v + step // 8 * i

        def bank(s, b):
            return 4 * s + b

        def cut_out(eng, cut, l, chunk):
            k = (chunk - OUT_C) % KT
            if chunk - OUT_C == 0:
                eng.wait_ge(yb_ready, l + 1)
            if chunk - OUT_C == 4:
                eng.wait_ge(yc_ready, l + 1)
            if chunk - OUT_C == 8:
                eng.wait_ge(ya_ready, 4 * l + 4)
            cut(l, chunk, k=k, gain=par[:, Q_MIXG + k:Q_MIXG + k + 1])

        @block.sync
        def _(sp):
            def load(l, p, src, i=None, step=0):
                last_chunk = 2 * (p - RING) + 1
                v = LAPS * l + last_chunk // RING + 1 + CREDIT
                sp.wait_ge(lo_cut[last_chunk % RING], v if i is None else v + 2 * step // RING * i)
                sp.sem_inc(slots_seen, 1)
                a = src.shape[0] // P
                dst = raw[:, p % RING, :].rearrange("p (a n) -> p a n", a=a)
                sp.dma_start(dst, src.rearrange("(a p) n -> p a n", p=P)).then_inc(panel_landed[p % RING], 16)

            for tt in range(TT):
                sp.dma_start(resid[:, tt, :], x[0, tt * P:tt * P + P, :]).then_inc(x_in[tt], 16)
            with sp.Fori(0, DEPTH) as l:
                wi, wo, wg, wu, wd = (w.rearrange("l k n -> (l k) n") for w in (w_in, w_out, w_gate, w_up, w_down))
                for g, col in enumerate(MIX_COLS):
                    for q in range(4):
                        load(l, 4 * g + q, wi[bass.ds(D * l + 512 * q, 512), col:col + 512])
                for half in range(2):
                    for p in range(KT // 2):
                        row = 2 * P * ((p + 4) % 8)
                        load(l, OUT_C // 2 + 8 * half + p,
                             wo[bass.ds(D * l + row, 2 * P), 1024 * half:1024 * half + 1024])
                with sp.Fori(0, N_PAIR) as i:
                    for u, w in enumerate((wg, wu)):
                        for q in range(4):
                            load(l, FFN_C // 2 + 4 * u + q,
                                 w[bass.ds(D * l + 512 * q, 512), bass.ds(512 * i, 512)], i, 8)
                for half in range(2):
                    first = DOWN_C // 2 + half * FT // 2
                    cols = slice(1024 * half, 1024 * half + 1024)
                    for p in range(2):
                        load(l, first + p, wd[bass.ds(D_FF * l + 2 * P * p, 2 * P), cols])
                    with sp.Fori(0, (FT // 2 - 2) // 4) as i:
                        for p in range(2, 6):
                            load(l, first + p, wd[bass.ds(D_FF * l + 8 * P * i + 2 * P * p, 2 * P), cols], i, 4)
            for n in range(4):
                tt, c = n // 2, (n % 2) * 1024
                sp.wait_ge(fin_b, n + 1)
                sp.dma_start(out[0, tt * P:tt * P + P, c:c + 1024], resid[:, tt, c:c + 1024]).then_inc(stored, 16)
            sp.wait_ge(stored, 64)

        @block.tensor
        def _(pe):
            def wait_chunk(l, c, i=None, step=0):
                pe.wait_ge(lo_cut[c % RING], lap(l, c, i, step) + CREDIT)

            def column_chunk(l, s, c0, c, i=None, step=0):
                wait_chunk(l, c0 + c, i, step)
                slot = c % RING
                for kk in range(2):
                    k = 2 * c + kk
                    for t in range(4):
                        w = slice(512 * kk + P * t, 512 * kk + P * t + P)
                        T.matmul(ps[:, bank(s, t), :], w_hi[:, slot, w], xT[:, k, :], start=(k == 0), stop=False)
                        last = T.matmul(ps[:, bank(s, t), 0:S], w_lo[:, slot, w], xT[:, k, 0:S],
                                        start=False, stop=(k == KT - 1))
                last.then_inc(used[slot], 1)

            def row_chunk(l, s, c, first, final, i=None, step=0):
                wait_chunk(l, c, i, step)
                slot = c % RING
                for cb in range(2):
                    for tt in range(TT):
                        o = ps[:, bank(s, 2 * tt + cb), :]
                        tok, col = slice(P * tt, P * tt + P), slice(512 * cb, 512 * cb + 512)
                        T.matmul(o, m_hi[:, slot, tok], w_hi[:, slot, col], start=first, stop=False)
                        T.matmul(o, m_hi[:, slot, tok], w_lo[:, slot, col], start=False, stop=False)
                        last = T.matmul(o, m_lo[:, slot, tok], w_hi[:, slot, col], start=False, stop=final)
                        if final and (cb, tt) != (1, 1):
                            last.then_inc(bank_done, 1)
                last.then_inc(used[slot], 1)

            def transposes(n, s, q):
                pe.wait_ge(norm0, 4 * n + q + 1)
                pe.wait_ge(norm1, 4 * n + q + 1)
                if q >= 2:
                    pe.wait_ge(xf_ready, 16 * n + 4 * (q - 2) + 4)
                for kk in range(4):
                    for tt in range(TT):
                        o = ps[:, bank(s, 2 * (q % 2) + kk // 2), S * (kk % 2) + P * tt:S * (kk % 2) + P * tt + P]
                        k = 4 * q + kk
                        last = T.transpose(o, resid[:, tt, P * k:P * k + P], ident)
                    if kk % 2:
                        last.then_inc(transposed, 1)

            def first_column_group(l, n, s, c0):
                transposes(n, 1 - s, 0)
                transposes(n, 1 - s, 1)
                for c in range(8):
                    if c in (2, 4):
                        transposes(n, 1 - s, 1 + c // 2)
                    pe.wait_ge(xT_ready, 8 * n + c + 1)
                    column_chunk(l, s, c0, c)

            pe.wait_ge(consts_in, 16)
            for slot in range(RING):
                pe.sem_inc(used[slot], CREDIT)
            with pe.Fori(0, DEPTH) as l:
                first_column_group(l, 2 * l, 1, 0)
                for g in range(1, N_MIX):
                    s = (g + 1) % 2
                    if g in (5, 6, 7):
                        pe.wait_ge(sums_out, 2 * N_COLG * l + 2 * (g - 2) + 2)
                    if g == 2:
                        pe.wait_ge(uv_act, l + 1)
                        pe.wait_ge(uv_dve, l + 1)
                    if g == 3:
                        pe.wait_ge(fr_act, l + 1)
                        pe.wait_ge(fr_dve, l + 1)
                    if g == 4:
                        pe.wait_ge(yb_ready, l + 1)
                        pe.wait_ge(yc_ready, l + 1)
                    if g == 5:
                        pe.wait_ge(ms_pf_ready, l + 1)
                    for c in range(8):
                        if c == 4 and g == 1:
                            pe.wait_ge(tables_in, 16)
                            pe.wait_ge(sums_out, 2 * N_COLG * l + 2)
                            for h in range(4):
                                for tt in range(TT):
                                    last = T.matmul(ps[:, 4 + h, S * tt:S * tt + S], zf[:, h, P * tt:P * tt + P],
                                                    dft_c, start=True, stop=True)
                            last.then_inc(uv_done, 1)
                        if c == 4 and g == 2:
                            pe.wait_ge(uv_act, l + 1)
                            pe.wait_ge(uv_dve, l + 1)
                            pe.wait_ge(sums_out, 2 * N_COLG * l + 4)
                            for h in range(4):
                                for n in range(4):
                                    tt, part = n // 2, n % 2
                                    last = T.matmul(ps[:, h // 2, S * (h % 2):S * (h % 2) + S],
                                                    uv[:, h, tt, P * part:P * part + P],
                                                    dft_s[:, tt, S * part:S * part + S], start=(n == 0), stop=(n == 3))
                            last.then_inc(fr_done, 1)
                        if c == 4 and g == 3:
                            pe.wait_ge(fr_act, l + 1)
                            pe.wait_ge(fr_dve, l + 1)
                            pe.wait_ge(pooled, l + 1)
                            pe.wait_ge(small_w_in, 16 * l + 16)
                            pe.wait_ge(sums_out, 2 * N_COLG * l + 6)
                            for h in range(8):
                                rhs = zf[:, h, :] if h < 4 else zp[:, h - 4, PAD:PAD + S]
                                last = T.matmul(ps[:, 4 + h // 2, S * (h % 2):S * (h % 2) + S], sw[:, h, :], rhs,
                                                start=True, stop=True)
                            last.then_inc(proj_done, 1)
                        if c == 4 and g == 4:
                            pe.wait_ge(ssq_pf, l + 1)
                            pe.wait_ge(sums_out, 2 * N_COLG * l + 8)
                            for r in range(2):
                                for tt in range(TT):
                                    last = T.matmul(ps[:, 0, 2 * r + tt:2 * r + tt + 1], ssq[:, r, P * tt:P * tt + P],
                                                    ones_pool, start=True, stop=True)
                            last.then_inc(ms_pf_done, 1)
                        column_chunk(l, s, 8 * g, c)
                for r in range(6):
                    s, (k0, kn, _) = 1 - r % 2, OUT_PARTS[r % 3]
                    base = OUT_C + KT * (r // 3) + k0
                    if r < 2:
                        pe.wait_ge(sums_out, 2 * N_COLG * l + 2 * (6 + r) + 2)
                    else:
                        pe.wait_ge(y_added, 32 * l + 4 * (r - 2) + 4)
                    if r == 2:
                        pe.wait_ge(ms_a_ready, l + 1)
                    for c in range(kn):
                        if r == 1 and c == 3:
                            pe.wait_ge(ssq_a, 2 * l + 2)
                            pe.wait_ge(y_added, 32 * l + 4)
                            for tt in range(TT):
                                last = T.matmul(ps[:, 4, tt:tt + 1], ssq[:, 2, P * tt:P * tt + P], ones_conv,
                                                start=True, stop=True)
                            last.then_inc(ms_a_done, 1)
                        row_chunk(l, s, base + c, c == 0, c == kn - 1)
                first_column_group(l, 2 * l + 1, 0, FFN_C)
                pe.wait_ge(xf_ready, 16 * (2 * l + 1) + 16)
                for c in range(8):
                    column_chunk(l, 1, FFN_C + 8, c)
                with pe.Fori(0, N_PAIR - 1) as i:
                    for u in range(2):
                        pe.wait_ge(sums_out, 2 * N_COLG * l + 2 * (N_MIX + u) + 2 + 4 * i)
                        for c in range(8):
                            column_chunk(l, u, FFN_C + 16 + 8 * u, c, i, 16)
                for half in range(2):
                    base = DOWN_C + FT * half
                    pe.wait_ge(sums_out, 2 * N_COLG * l + 2 * (N_COLG - 2 + half) + 2)
                    for c in range(4):
                        row_chunk(l, half, base + c, c == 0, False)
                    with pe.Fori(0, FT // 4 - 2) as i:
                        for c in range(4):
                            row_chunk(l, half, base + 4 + c, False, False, i, 4)
                    for c in range(FT - 4, FT):
                        row_chunk(l, half, base + c, False, c == FT - 1)

        @block.scalar
        def _(act):
            def cut_hi(l, c, i=None, step=0, k=None, gain=1.0):
                slot = c % RING
                act.wait_ge(used[slot], lap(l, c, i, step) - 1 + CREDIT)
                if k is not None:
                    A.activation(m_hi[:, slot, :], feat[:, k, :], ACT.Copy, scale=gain)
                act.wait_ge(panel_landed[c // 2 % RING], 16 * plap(l, c, i, step))
                A.activation(w_hi[:, slot, :], raw[:, c // 2 % RING, 1024 * (c % 2):1024 * (c % 2) + 1024],
                             ACT.Copy).then_inc(hi_cut[slot], 1)

            def copy_low(l, g, st, c_last, i=None, pair=0):
                s = (g + 1) % 2 if g < N_MIX else (g - N_MIX) % 2
                if st == 0:
                    act.wait_ge(used[3], lap(l, c_last, i, 16 if i is not None else 0) + CREDIT)
                A.activation(low[:, 2 * st:2 * st + 2, :], ps[:, bank(s, 2 * st):bank(s, 2 * st) + 2, S:2 * S],
                             ACT.Copy).then_inc(low_copied, 1)

            def centre_tap(tile, w, b, done):
                A.activation(mid[:, tile, :], padded[:, tile, 1:S + 1], ACT.Identity, bias=b, scale=w).then_inc(done, 1)

            def norm_rows(n, q):
                A.activation(resid[:, 1, 512 * q:512 * q + 512], resid[:, 1, 512 * q:512 * q + 512], ACT.Identity,
                             bias=nmr[:, 1:2], scale=rstd[:, 1:2]).then_inc(norm1, 1)

            def read_transposed(n, s, q, qg, qb):
                if q >= 2:
                    act.wait_ge(xT_ready, 8 * n + 2 * (q - 2) + 2)
                for kk in range(4):
                    k = 4 * q + kk
                    if kk % 2 == 0:
                        act.wait_ge(transposed, 8 * n + k // 2 + 1)
                    A.activation(xf[:, q % 2, kk, :], ps[:, bank(s, 2 * (q % 2) + kk // 2), S * (kk % 2):S * (kk % 2) + S],
                                 ACT.Identity, bias=par[:, qb + k:qb + k + 1],
                                 scale=par[:, qg + k:qg + k + 1]).then_inc(xf_ready, 1)

            def behind_norm(l, n, s, c0, qg, qb):
                for c in range(AHEAD):
                    cut_hi(l, c0 + c)
                act.wait_ge(nmr_ready, n + 1)
                norm_rows(n, 0)
                norm_rows(n, 1)
                act.wait_ge(params_in, 16 * l + 16)
                read_transposed(n, 1 - s, 0, qg, qb)
                norm_rows(n, 2)
                norm_rows(n, 3)
                read_transposed(n, 1 - s, 1, qg, qb)
                for c in range(8):
                    cut_hi(l, c0 + c + AHEAD)
                    if c in (2, 4):
                        read_transposed(n, 1 - s, 1 + c // 2, qg, qb)
                    if c == 5 and s == 1:
                        act.dma_start(sw[:, :, :].rearrange("p a n -> p (a n)"),
                                      small_w[bass.ds(P * l, P), :]).then_inc(small_w_in, 16)
                        for r, dst in enumerate((ln_g, ln_b)):
                            act.dma_start(dst, ln_rows[bass.ds(4 * l + r, 1), :].to_broadcast([P, D])).then_inc(ln_rows_in, 16)

            def gate_hooks(c, l, i, c_last, tile0):
                n_before = 4 * N_PAIR * l + 4 * i if i is not None else 4 * N_PAIR * l + 4 * (N_PAIR - 1)
                g = N_MIX
                if c in (0, 1):
                    copy_low(l, g, c, c_last, i)
                if c in (1, 2):
                    v = 2 * N_COLG * l + 2 * N_MIX
                    v = v + 4 * i if i is not None else v + 4 * (N_PAIR - 1)
                    act.wait_ge(sums_out, v + c)
                    for t in (2 * c - 2, 2 * c - 1):
                        centre_tap(t, par[:, fcol(Q_FCW + FT, tile0, t)], par[:, fcol(Q_FCB, tile0, t)], g_mid)
                if c in (3, 4):
                    if c == 3:
                        act.wait_ge(resid_ready, 2 * l + 2)
                    for t in (2 * c - 6, 2 * c - 5):
                        act.wait_ge(g_conv, n_before + t + 1)
                        A.activation(feat[:, fcol(0, tile0, t), :], conv[:, t:t + 1, :], ACT.Gelu).then_inc(gelu_done, 1)

            def fcol(base, tile0, t):
                return bass.ds(tile0 + (base + t), 1)

            act.dma_start(cst[:, 0:K_DFTC], consts[:, 0:K_DFTC]).then_inc(consts_in, 16)
            act.wait_ge(panel_landed[0], 16)
            act.dma_start(cst[:, K_DFTC:NCONST], consts[:, K_DFTC:NCONST]).then_inc(tables_in, 16)

            with act.Fori(0, DEPTH) as l:
                act.dma_start(par[:, :], params[bass.ds(P * l, P), :]).then_inc(params_in, 16)
                behind_norm(l, 2 * l, 1, 0, Q_LNA_G, Q_LNA_B)
                for g in range(1, N_MIX + 1):
                    for c in range(8):
                        chunk = 8 * g + c + AHEAD
                        if g == N_MIX:
                            break
                        if chunk >= OUT_C:
                            cut_out(act, cut_hi, l, chunk)
                        else:
                            cut_hi(l, chunk)
                        if c in (0, 1):
                            copy_low(l, g - 1, c, 8 * g - 1)
                        if g in (4, 7) and c in (2, 3):
                            act.wait_ge(cv_ready, 4 * l + 2 * (g // 6) + c - 1)
                            for t in (2 * c - 4, 2 * c - 3):
                                q = Q_CONV + CONV_TILES + 4 * (g // 6) + t
                                centre_tap(t, par[:, q:q + 1], 0.0, mid_ready)
                        if c == 4 and g == 1:
                            act.wait_ge(uv_done, l + 1)
                            A.activation(uv[:, 0:2, :, :].rearrange("p h t c -> p h (t c)"), ps[:, 4:6, :], ACT.Copy).then_inc(uv_act, 1)
                        if c == 4 and g == 2:
                            act.wait_ge(fr_done, l + 1)
                            A.activation(zf[:, 0:2, :], ps[:, 0, :].rearrange("p (a s) -> p a s", a=2), ACT.Copy).then_inc(fr_act, 1)
                        if c == 4 and g == 3:
                            act.wait_ge(proj_done, l + 1)
                            for t in range(4):
                                last = A.activation(feat[:, t, :], ps[:, 6 + t // 2, S * (t % 2):S * (t % 2) + S], ACT.Copy,
                                                    scale=par[:, Q_PSC + t:Q_PSC + t + 1])
                            last.then_inc(yb_ready, 1)
                        if c == 4 and g == 5:
                            act.wait_ge(resid_ready, 2 * l + 1)
                            for r, dst in enumerate((ln_g, ln_b)):
                                act.dma_start(dst, ln_rows[bass.ds(2 * (2 * l + 1) + r, 1), :].to_broadcast([P, D])).then_inc(ln_rows_in, 16)
                for c in range(2 * KT):
                    if c + AHEAD < 2 * KT:
                        cut_out(act, cut_hi, l, OUT_C + c + AHEAD)
                    if c in (0, 1):
                        copy_low(l, N_MIX - 1, c, OUT_C - 1)
                behind_norm(l, 2 * l + 1, 0, FFN_C, Q_LN1_G, Q_LN1_B)
                with act.Fori(0, N_PAIR - 1) as i:
                    for c in range(8):
                        cut_hi(l, FFN_C + 8 + c + AHEAD, i, 16)
                        gate_hooks(c, l, i, FFN_C + 7, 4 * i)
                    for c in range(8):
                        cut_hi(l, FFN_C + 16 + c + AHEAD, i, 16)
                        if c in (0, 1):
                            copy_low(l, N_MIX + 1, c, FFN_C + 15, i)
                for c in range(8):
                    chunk = DOWN_C - 8 + c + AHEAD
                    if chunk >= DOWN_C:
                        cut_hi(l, chunk, k=chunk - DOWN_C)
                    else:
                        cut_hi(l, chunk)
                    gate_hooks(c, l, None, DOWN_C - 9, 4 * (N_PAIR - 1))
                for half in range(2):
                    base = DOWN_C + FT * half
                    for c in range(8):
                        if half == 0 and c == 2:
                            act.wait_ge(h_ready, 2 * N_PAIR * l + 2 * N_PAIR)
                        cut_hi(l, base + c + AHEAD, k=c + AHEAD)
                        if half == 0 and c in (0, 1):
                            copy_low(l, N_COLG - 1, c, DOWN_C - 1)
                    with act.Fori(0, FT // 8 - 1) as i:
                        for c in range(8):
                            cut_hi(l, base + 8 + c + AHEAD, i, 8, k=bass.ds(8 * i + (8 + c + AHEAD), 1))
                    for c in range(FT - 4, FT):
                        if c + AHEAD < FT or half == 0:
                            cut_hi(l, base + c + AHEAD, k=(c + AHEAD) % FT)

        @block.vector
        def _(dve):
            def cut_lo(l, c, i=None, step=0, k=None, gain=None):
                slot = c % RING
                dve.wait_ge(hi_cut[slot], lap(l, c, i, step))
                if gain is not None:
                    V.scalar_tensor_tensor(out=m_lo[:, slot, :], in0=feat[:, k, :], scalar=gain,
                                           in1=m_hi[:, slot, :].bitcast(F32), op0=ALU.mult, op1=ALU.subtract)
                elif k is not None:
                    V.tensor_tensor(m_lo[:, slot, :], feat[:, k, :], m_hi[:, slot, :].bitcast(F32), ALU.subtract)
                V.tensor_tensor(w_lo[:, slot, :], raw[:, c // 2 % RING, 1024 * (c % 2):1024 * (c % 2) + 1024],
                                w_hi[:, slot, :].bitcast(F32), ALU.subtract).then_inc(lo_cut[slot], 1)

            def add_halves(l, g, st, dst, i=None):
                s = (g + 1) % 2 if g < N_MIX else (g - N_MIX) % 2
                v = 2 * N_COLG * l + 2 * g + st + 1
                dve.wait_ge(low_copied, v if i is None else v + 4 * i)
                V.tensor_tensor(dst, ps[:, bank(s, 2 * st):bank(s, 2 * st) + 2, 0:S], low[:, 2 * st:2 * st + 2, :],
                                ALU.add).then_inc(sums_out, 1)

            def after_sum(l, g, st, i=None):
                v = 2 * N_COLG * l + 2 * g + st + 1
                dve.wait_ge(sums_out, v if i is None else v + 4 * i)

            def add_row_bank(l, r, s, j):
                cb, tt = j // 2, j % 2
                if j < 3:
                    dve.wait_ge(bank_done, 24 * l + 3 * r + j + 1)
                else:
                    last_chunk = (OUT_C + KT * (r // 3) + sum(OUT_PARTS[r % 3][:2]) if r < 6 else DOWN_C + FT * (r - 5)) - 1
                    dve.wait_ge(used[3], lap(l, last_chunk) + CREDIT)
                half = r // 3 if r < 6 else r - 6
                y = resid[:, tt, 1024 * half + 512 * cb:1024 * half + 512 * cb + 512]
                factor = rms[:, r % 3, tt:tt + 1] if r < 6 else 1.0 / ALPHA
                if r < 6 and r % 3:
                    dve.wait_ge(y_added, 32 * l + 4 * (r - 1) + j + 1)
                V.scalar_tensor_tensor(out=y, in0=ps[:, bank(s, 2 * tt + cb), :], scalar=factor, in1=y,
                                       op0=ALU.mult, op1=ALU.add).then_inc(y_added, 1)
                if r in (2, 5, 6, 7):
                    dve.wait_ge(y_added, 32 * l + 4 * r + j + 1)
                    V.bn_stats(stats[:, tt, 2 * half + cb, :], y).then_inc(stats_done, 1)

            def n_in_layer(c0):
                return 1 if c0 else 0

            def mean_var(n):
                dve.wait_ge(stats_done, 8 * n + 8)
                V.memset(pin[:, :], 0.0)
                for tt in range(TT):
                    last = V.bn_aggr(mv[:, tt, :], stats[:, tt, :, :].rearrange("p a b -> p (a b)"))
                last.then_inc(mv_done, 1)
                dve.wait_ge(mv_done, n + 1)
                V.tensor_scalar(var_eps[:, :], mv[:, :, 1], norm_eps[:, 0:1], None, ALU.add).then_inc(var_ready, 1)

            def cut_x(n, p):
                q, kk = p // 2, 2 * (p % 2)
                src = xf[:, q % 2, kk:kk + 2, :]
                dve.wait_ge(xf_ready, 16 * n + 2 * p + 2)
                V.tensor_copy(xT[:, 2 * p:2 * p + 2, 0:S], src).then_inc(xT_hi, 1)
                dve.wait_ge(xT_hi, 8 * n + p + 1)
                V.tensor_tensor(xT[:, 2 * p:2 * p + 2, S:2 * S], src, xT[:, 2 * p:2 * p + 2, 0:S].bitcast(F32),
                                ALU.subtract).then_inc(xT_ready, 1)

            def behind_norm(l, n, c0):
                dve.wait_ge(eps_set, l + 1 + n_in_layer(c0))
                mean_var(n)
                cut_lo(l, c0)
                dve.wait_ge(rstd_ready, n + 1)
                if c0 == 0:
                    V.memset(norm_eps[:, :], LN_EPS / ALPHA ** 2).then_inc(eps_set, 1)
                V.scalar_tensor_tensor(out=nmr[:, :], in0=mv[:, :, 0], scalar=-1.0, in1=rstd[:, :],
                                       op0=ALU.mult, op1=ALU.mult).then_inc(nmr_ready, 1)
                for q in range(4):
                    y = resid[:, 0, 512 * q:512 * q + 512]
                    V.tensor_scalar(y, y, mv[:, 0, 0:1], rstd[:, 0:1], ALU.subtract, ALU.mult).then_inc(norm0, 1)
                cut_x(n, 0)
                cut_x(n, 1)
                cut_lo(l, c0 + 1)
                cut_x(n, 2)
                cut_x(n, 3)
                cut_lo(l, c0 + 2)
                for c in range(8):
                    cut_lo(l, c0 + c + AHEAD)
                    if c in (2, 4):
                        cut_x(n, 2 + c)
                        cut_x(n, 3 + c)

            def outer_taps(t, w0, w2, mid_sem, n_mid, tap_sem, n_tap, done):
                for u in (t, t + 1):
                    dve.wait_ge(mid_sem, n_mid + u + 1)
                    V.scalar_tensor_tensor(out=conv[:, u, :], in0=padded[:, u, 0:S], scalar=w0(u), in1=mid[:, u, :],
                                           op0=ALU.mult, op1=ALU.add).then_inc(tap_sem, 1)
                for u in (t, t + 1):
                    dve.wait_ge(tap_sem, n_tap + u + 1)
                    V.scalar_tensor_tensor(out=conv[:, u, :], in0=padded[:, u, 2:S + 2], scalar=w2(u), in1=conv[:, u, :],
                                           op0=ALU.mult, op1=ALU.add).then_inc(done, 1)

            def gate_hooks(c, l, i, g, tile0):
                if c in (0, 1):
                    add_halves(l, g, c, padded[:, 2 * c:2 * c + 2, 1:S + 1], i)
                if c in (2, 3):
                    n = 4 * N_PAIR * l + (4 * i if i is not None else 4 * (N_PAIR - 1))
                    outer_taps(2 * c - 4, lambda u: par[:, bass.ds(tile0 + (Q_FCW + u), 1)],
                               lambda u: par[:, bass.ds(tile0 + (Q_FCW + 2 * FT + u), 1)], g_mid, n, g_tap0, n, g_conv)

            def up_hooks(c, l, i, g, tile0):
                if c in (0, 1):
                    add_halves(l, g, c, conv[:, 2 * c:2 * c + 2, :], i)
                    after_sum(l, g, c, i)
                    h = feat[:, bass.ds(tile0 + 2 * c, 2), :]
                    V.tensor_tensor(h, h, conv[:, 2 * c:2 * c + 2, :], ALU.mult).then_inc(h_ready, 1)

            def conv_output(l, grp, g, st):
                t = 8 + 4 * grp + 2 * st
                add_halves(l, g, st, feat[:, t:t + 2, :])
                after_sum(l, g, st)
                V.tensor_tensor(feat[:, t:t + 2, :], feat[:, t:t + 2, :], conv[:, 2 * st:2 * st + 2, :],
                                ALU.mult).then_inc(ya_ready, 1)

            for slot in range(RING):
                dve.sem_inc(lo_cut[slot], CREDIT)
            V.memset(norm_eps[:, :], LN_EPS).then_inc(eps_set, 1)
            V.memset(neg_half[:, :], -0.5).then_inc(neg_half_set, 1)
            V.memset(padded[:, :, :], 0.0).then_inc(pads_zero, 1)
            for tt in range(TT):
                dve.wait_ge(x_in[tt], 16)
                for q in range(4):
                    V.bn_stats(stats[:, tt, q, :], resid[:, tt, 512 * q:512 * q + 512]).then_inc(stats_done, 1)
            dve.wait_ge(pads_zero, 1)
            with dve.Fori(0, DEPTH) as l:
                behind_norm(l, 2 * l, 0)
                dve.wait_ge(params_in, 16 * l + 16)
                for g in range(1, N_MIX):
                    for c in range(8):
                        chunk = 8 * g + c + AHEAD
                        if chunk >= OUT_C:
                            cut_out(dve, cut_lo, l, chunk)
                        else:
                            cut_lo(l, chunk)
                        two = slice(2 * c, 2 * c + 2)
                        if c in (0, 1):
                            if g == 1:
                                add_halves(l, 0, c, zf[:, two, :])
                            if g == 2:
                                if c == 0:
                                    dve.wait_ge(resid_ready, 2 * l + 1)
                                    V.memset(zp[:, :, 0:PAD], 0.0)
                                    V.memset(zp[:, :, PAD + S:W], 0.0)
                                add_halves(l, 1, c, zp[:, two, PAD:PAD + S])
                            if g in (3, 6):
                                add_halves(l, g - 1, c, conv[:, two, :])
                            if g in (4, 7):
                                add_halves(l, g - 1, c, padded[:, two, 1:S + 1])
                                after_sum(l, g - 1, c)
                                V.tensor_tensor(padded[:, two, 1:S + 1], padded[:, two, 1:S + 1], conv[:, two, :],
                                                ALU.mult).then_inc(cv_ready, 1)
                            if g == 5:
                                conv_output(l, 0, 4, c)
                        if g in (4, 7) and c in (3, 4):
                            grp = g // 6
                            q = Q_CONV + 4 * grp
                            n = 8 * l + 4 * grp
                            outer_taps(2 * c - 6, lambda u: par[:, q + u:q + u + 1],
                                       lambda u: par[:, q + 2 * CONV_TILES + u:q + 2 * CONV_TILES + u + 1],
                                       mid_ready, n, tap0, n, conv_done)
                        if c == 4 and g == 1:
                            dve.wait_ge(uv_done, l + 1)
                            V.tensor_copy(uv[:, 2:4, :, :].rearrange("p h t c -> p h (t c)"), ps[:, 6:8, :]).then_inc(uv_dve, 1)
                        if c == 4 and g == 2:
                            dve.wait_ge(fr_done, l + 1)
                            V.tensor_copy(zf[:, 2:4, :], ps[:, 1, :].rearrange("p (a s) -> p a s", a=2)).then_inc(fr_dve, 1)
                        if c == 4 and g == 3:
                            dve.wait_ge(proj_done, l + 1)
                            V.tensor_copy(feat[:, 4:8, :], ps[:, 4:6, :].rearrange("p b (a s) -> p (b a) s", a=2)).then_inc(yc_ready, 1)
                        if c == 5 and g == 4:
                            dve.wait_ge(ms_pf_done, l + 1)
                            V.tensor_scalar(ms[:, 0:2, :], ps[:, 0, 0:2 * TT].rearrange("p (a t) -> p a t", a=2), RMS_EPS,
                                            ALPHA * ALPHA, ALU.add, ALU.mult).then_inc(ms_pf_ready, 1)
                for c in range(2 * KT):
                    if c + AHEAD < 2 * KT:
                        cut_out(dve, cut_lo, l, OUT_C + c + AHEAD)
                    if c in (0, 1):
                        conv_output(l, 1, N_MIX - 1, c)
                    if c == 7:
                        dve.wait_ge(ms_a_done, l + 1)
                        V.tensor_scalar(ms[:, 2, :], ps[:, 4, 0:TT], RMS_EPS, ALPHA * ALPHA, ALU.add,
                                        ALU.mult).then_inc(ms_a_ready, 1)
                    for r in range(5):
                        first = KT * ((r + 1) // 3) + OUT_PARTS[(r + 1) % 3][0]
                        if c in (first, first + 1):
                            if c == first and r == 0:
                                dve.wait_ge(rms_pf, l + 1)
                            if c == first and r == 2:
                                dve.wait_ge(rms_a, l + 1)
                            for j in (2 * (c - first), 2 * (c - first) + 1):
                                add_row_bank(l, r, 1 - r % 2, j)
                for j in range(4):
                    add_row_bank(l, 5, 0, j)
                behind_norm(l, 2 * l + 1, FFN_C)
                with dve.Fori(0, N_PAIR - 1) as i:
                    for c in range(8):
                        cut_lo(l, FFN_C + 8 + c + AHEAD, i, 16)
                        gate_hooks(c, l, i, N_MIX, 4 * i)
                    for c in range(8):
                        cut_lo(l, FFN_C + 16 + c + AHEAD, i, 16)
                        up_hooks(c, l, i, N_MIX + 1, 4 * i)
                for c in range(8):
                    chunk = DOWN_C - 8 + c + AHEAD
                    if chunk >= DOWN_C:
                        if chunk == DOWN_C:
                            dve.wait_ge(h_ready, 2 * N_PAIR * l + 2 * N_PAIR - 2)
                        cut_lo(l, chunk, k=chunk - DOWN_C)
                    else:
                        cut_lo(l, chunk)
                    gate_hooks(c, l, None, N_COLG - 2, 4 * (N_PAIR - 1))
                for half in range(2):
                    base = DOWN_C + FT * half
                    for c in range(8):
                        if half == 0 and c == 2:
                            dve.wait_ge(h_ready, 2 * N_PAIR * l + 2 * N_PAIR)
                        cut_lo(l, base + c + AHEAD, k=c + AHEAD)
                        if half == 0:
                            up_hooks(c, l, None, N_COLG - 1, 4 * (N_PAIR - 1))
                        elif c in (0, 1):
                            for j in (2 * c, 2 * c + 1):
                                add_row_bank(l, 6, 0, j)
                    with dve.Fori(0, FT // 8 - 1) as i:
                        for c in range(8):
                            cut_lo(l, base + 8 + c + AHEAD, i, 8, k=bass.ds(8 * i + (8 + c + AHEAD), 1))
                    for c in range(FT - 4, FT):
                        if c + AHEAD < FT or half == 0:
                            cut_lo(l, base + c + AHEAD, k=(c + AHEAD) % FT)
                for j in range(4):
                    add_row_bank(l, 7, 1, j)
            n = 2 * DEPTH
            dve.wait_ge(eps_set, DEPTH + 1)
            mean_var(n)
            dve.wait_ge(rstd_ready, n + 1)
            dve.wait_ge(last_rows_in, 32)
            for j in range(4):
                tt, c = j // 2, (j % 2) * 1024
                y = resid[:, tt, c:c + 1024]
                V.scalar_tensor_tensor(out=y, in0=y, scalar=mv[:, tt, 0:1], in1=ln_g[:, c:c + 1024],
                                       op0=ALU.subtract, op1=ALU.mult).then_inc(fin_a, 1)
                dve.wait_ge(fin_a, j + 1)
                V.scalar_tensor_tensor(out=y, in0=y, scalar=rstd[:, tt:tt + 1], in1=ln_b[:, c:c + 1024],
                                       op0=ALU.mult, op1=ALU.add).then_inc(fin_b, 1)

        @block.gpsimd
        def _(pool):
            def power(src, dst, width, ready, n, done):
                pool.wait_ge(ready, n)
                G.tensor_tensor(dst, src, neg_half[:, 0:width], ALU.pow).then_inc(done, 1)

            def make_residual(n):
                pool.wait_ge(ln_rows_in, 32 * n + 32)
                pool.wait_ge(transposed, 8 * n + 8)
                for tt in range(TT):
                    G.tensor_tensor(resid[:, tt, :], resid[:, tt, :], ln_g, ALU.mult).then_inc(resid_scaled, 1)
                for tt in range(TT):
                    pool.wait_ge(resid_scaled, 2 * n + tt + 1)
                    last = G.tensor_tensor(resid[:, tt, :], resid[:, tt, :], ln_b, ALU.add)
                last.then_inc(resid_ready, 1)

            pool.wait_ge(neg_half_set, 1)
            pool.wait_ge(tables_in, 16)
            with pool.Fori(0, DEPTH) as l:
                power(var_eps[:, :], rstd[:, :], TT, var_ready, 2 * l + 1, rstd_ready)
                make_residual(2 * l)
                pool.wait_ge(sums_out, 2 * N_COLG * l + 4)
                src, lo_edge, hi_edge = zp, 0, W
                for lev, half in enumerate(POOL_HALF):
                    sh = max(half // 2, 0)
                    dst = win[lev % 2]
                    if lev == 0:
                        lo_edge = 1
                        a, b = zp[:, :, 0:W - 1], zp[:, :, 1:W]
                        o = dst[:, :, 1:W]
                    else:
                        lo_edge, hi_edge = lo_edge + sh, hi_edge - sh
                        a = src[:, lev:4, lo_edge - sh:hi_edge - sh]
                        b = src[:, lev:4, lo_edge + sh:hi_edge + sh]
                        o = dst[:, lev:4, lo_edge:hi_edge]
                        pool.wait_ge(window, 9 * l + lev)
                    G.tensor_tensor(o, a, b, ALU.add).then_inc(window, 1)
                    src = dst
                pool.wait_ge(window, 9 * l + 4)
                for g in range(4):
                    o = win[g % 2][:, g, PAD:PAD + S]
                    G.tensor_tensor(o, o, inv_count[:, g, :], ALU.mult).then_inc(window, 1)
                for g in range(4):
                    pool.wait_ge(window, 9 * l + 5 + g)
                    last = G.tensor_tensor(zp[:, g, PAD:PAD + S], win[g % 2][:, g, PAD:PAD + S], zp[:, g, PAD:PAD + S],
                                           ALU.subtract)
                    if g == 0:
                        last.then_inc(window, 1)
                last.then_inc(pooled, 1)
                pool.wait_ge(yb_ready, l + 1)
                pool.wait_ge(yc_ready, l + 1)
                G.tensor_tensor(sq[:, :, :], feat[:, 0:8, :], feat[:, 0:8, :], ALU.mult).then_inc(sq_step, 1)
                sqv = sq.rearrange("p (g t) s -> p g t s", g=2)
                pool.wait_ge(sq_step, 2 * l + 1)
                G.tensor_tensor(sqv[:, :, 0:2, :], sqv[:, :, 0:2, :], sqv[:, :, 2:4, :], ALU.add).then_inc(sq_step, 1)
                pool.wait_ge(sq_step, 2 * l + 2)
                G.tensor_tensor(ssq[:, 0:2, :], sqv[:, :, 0, :], sqv[:, :, 1, :], ALU.add).then_inc(ssq_pf, 1)
                power(ms[:, 0:2, :].rearrange("p a t -> p (a t)"), rms[:, 0:2, :].rearrange("p a t -> p (a t)"), 2 * TT,
                      ms_pf_ready, l + 1, rms_pf)
                pool.wait_ge(ssq_pf, l + 1)
                for h in range(2):
                    y = feat[:, 8 + 4 * h:12 + 4 * h, :]
                    pool.wait_ge(ya_ready, 4 * l + 2 * h + 2)
                    G.tensor_tensor(sq[:, 0:4, :], y, y, ALU.mult).then_inc(sqa_step, 1)
                    pool.wait_ge(sqa_step, 5 * l + 2 * h + 1)
                    G.tensor_tensor(sq[:, 0:2, :], sq[:, 0:2, :], sq[:, 2:4, :], ALU.add).then_inc(sqa_step, 1)
                    pool.wait_ge(sqa_step, 5 * l + 2 * h + 2)
                    if h == 0:
                        G.tensor_tensor(ssq[:, 2, :], sq[:, 0, :], sq[:, 1, :], ALU.add).then_inc(ssq_a, 1)
                        pool.wait_ge(ssq_a, 2 * l + 1)
                    else:
                        G.tensor_tensor(sq[:, 0, :], sq[:, 0, :], sq[:, 1, :], ALU.add).then_inc(sqa_step, 1)
                        pool.wait_ge(sqa_step, 5 * l + 5)
                        G.tensor_tensor(ssq[:, 2, :], ssq[:, 2, :], sq[:, 0, :], ALU.add).then_inc(ssq_a, 1)
                power(ms[:, 2, :], rms[:, 2, :], TT, ms_a_ready, l + 1, rms_a)
                power(var_eps[:, :], rstd[:, :], TT, var_ready, 2 * l + 2, rstd_ready)
                make_residual(2 * l + 1)
            n = 2 * DEPTH
            pool.wait_ge(lo_cut[3], LAPS * DEPTH + CREDIT)
            for r, dst in enumerate((ln_g, ln_b)):
                pool.dma_start(dst, ln_rows[2 * n + r:2 * n + r + 1, :].to_broadcast([P, D])).then_inc(last_rows_in, 16)
            power(var_eps[:, :], rstd[:, :], TT, var_ready, n + 1, rstd_ready)


def kernel(**inputs):
    import numpy as np
    import concourse.bacc as bacc
    from concourse import mybir
    from concourse.bass_utils import run_bass_kernel_spmd as run

    f = np.float32
    a = {k: np.ascontiguousarray(v) for k, v in inputs.items()}

    def chan(v):
        return v.reshape(-1, v.shape[-1] // P, P).transpose(2, 0, 1).reshape(P, -1)

    def used_order(v):
        return np.concatenate([v[CONV:], v[:CONV]])

    ln_g = [a["ln_in_g"]] + [a[f"ln{j}_g"][l] for l in range(DEPTH) for j in (1, 2)]
    ln_b = [a["ln_in_b"]] + [a[f"ln{j}_b"][l] for l in range(DEPTH) for j in (1, 2)]
    params = np.concatenate([np.concatenate([
        chan(ln_g[2 * l]), chan(ln_b[2 * l]), chan(ln_g[2 * l + 1]), chan(ln_b[2 * l + 1]), chan(a["conv_a"][l]),
        chan(a["pool_scale"][l]), chan(used_order(a["mix_norm_g"][l])), chan(a["ffn_conv_w"][l]),
        chan(a["ffn_conv_b"][l])], axis=1) for l in range(DEPTH)])
    small_w = np.concatenate([np.concatenate([a["fourier_w"][l], a["pool_w"][l]]).transpose(1, 0, 2).reshape(P, -1)
                              for l in range(DEPTH)])
    ln_rows = np.stack([v for g, b in zip(ln_g, ln_b) for v in (g, b)])

    c, t = np.arange(P), np.arange(S)
    ang_c = 2 * np.pi * (np.outer(c, c) % P) / P
    ang_t = 2 * np.pi * (np.outer(t, t) % S) / S
    dft_c = np.concatenate([np.cos(ang_c), np.sin(ang_c)], axis=1) / np.sqrt(P)
    dft_t = np.concatenate([np.cos(ang_t), -np.sin(ang_t)], axis=1) / np.sqrt(S)
    inv = np.stack([1.0 / (np.minimum(t + h, S) - np.maximum(t - h, 0)) for h in POOL_HALF]).reshape(1, -1)
    consts = np.concatenate([np.eye(P), np.full((P, 1), 1 / POOLW), np.full((P, 1), 1 / CONV), dft_c,
                             np.broadcast_to(inv, (P, 4 * S)), dft_t[:P], dft_t[P:]], axis=1).astype(f)

    arrays = {"x": a["x"], "w_in": a["w_in"], "w_out": a["w_out"], "w_gate": a["w_gate"], "w_up": a["w_up"],
              "w_down": a["w_down"], "params": params, "small_w": small_w, "ln_rows": ln_rows, "consts": consts}
    nc = bacc.Bacc("TRN2", target_bir_lowering=False, num_devices=1)
    arrays = {k: np.ascontiguousarray(v) for k, v in arrays.items()}
    args = [nc.dram_tensor(k, v.shape, mybir.dt.from_np(v.dtype), kind="ExternalInput").ap() for k, v in arrays.items()]
    out = nc.dram_tensor("out", (1, S, D), mybir.dt.float32, kind="ExternalOutput").ap()
    build(nc, *args, out)
    return run(nc, [arrays], core_ids=[0]).results[0]["out"]
```

```python
import concourse.bass as bass
from concourse import mybir
from contextlib import ExitStack

P = 128
S = 256
TT = S // P
D = 2048
KT = D // P
DEPTH = 2
D_FF = 5632
FT = D_FF // P
ALPHA = (2.0 * DEPTH) ** 0.25
LN_EPS = 1e-5
RMS_EPS = 1e-6
CONV = D // 2
POOLW = D // 4
CONV_TILES = CONV // P
POOL_HALF = (1, 2, 4, 8)
PAD = 8

C_B, C_C, C_V = 0, CONV, 2 * CONV
C_POOL, C_FOUR = 3 * CONV, 3 * CONV + POOLW
MIX_COLS = [C_FOUR, C_POOL, C_C, C_V, C_B, C_C + 512, C_V + 512, C_B + 512]
N_MIX = len(MIX_COLS)
N_PAIR = FT // 4
N_COLG = N_MIX + 2 * N_PAIR

OUT_C = 8 * N_MIX
OUT_PARTS = [(0, 4, 0), (4, 4, 1), (8, 8, 2)]
FFN_C = OUT_C + 2 * KT
DOWN_C = FFN_C + 16 * N_PAIR
LAYER_C = DOWN_C + 2 * FT
RING = 4
AHEAD = 3
LAPS = LAYER_C // RING
PLAPS = LAYER_C // 2 // RING
CREDIT = 2

Q_LNA_G, Q_LNA_B, Q_LN1_G, Q_LN1_B = 0, KT, 2 * KT, 3 * KT
Q_CONV = 4 * KT
Q_PSC = Q_CONV + 3 * CONV_TILES
Q_MIXG = Q_PSC + 4
Q_FCW = Q_MIXG + KT
Q_FCB = Q_FCW + 3 * FT
NPAR = Q_FCB + FT
K_ID, K_ONE5, K_ONE10, K_DFTC = 0, P, P + 1, P + 2
K_INV = K_DFTC + 2 * P
K_DFTS = K_INV + 4 * S
NCONST = K_DFTS + 2 * S

LAST_POOL = [(0, 0, 512), (0, 512, 512), (0, 1024, 512)]
LAST_DVE = [(1, 0, 1024), (1, 1024, 1024), (0, 1536, 512)]


def build(nc, x, w_in, w_out, w_gate, w_up, w_down, params, small_w, ln_rows, consts, out):
    F32, F32R = mybir.dt.float32, mybir.dt.float32r
    ALU, ACT = mybir.AluOpType, mybir.ActivationFunctionType
    V, A, G, T = nc.vector, nc.scalar, nc.gpsimd, nc.tensor

    with ExitStack() as ctx:
        def sb(name, shape, dt=F32):
            return ctx.enter_context(nc.sbuf_tensor(name, shape, dt))

        def sem(name):
            return ctx.enter_context(nc.semaphore(name))

        resid = sb("resid", [P, TT, D])
        xT = sb("xT", [P, KT, 2 * S], F32R)
        feat = sb("feat", [P, FT, S])
        raw = sb("raw", [P, RING, 2048])
        w_hi = sb("w_hi", [P, RING, 1024], F32R)
        w_lo = sb("w_lo", [P, RING, 1024], F32R)
        m_hi = sb("m_hi", [P, RING, S], F32R)
        m_lo = sb("m_lo", [P, RING, S], F32R)
        scratch = sb("scratch", [P, 8, S])
        xf = scratch[:, :, :].rearrange("p (a k) s -> p a k s", a=2)
        low = scratch[:, 0:4, :]
        mid = scratch[:, 4:8, :]
        padded = sb("padded", [P, 4, S + 2])
        conv = sb("conv", [P, 4, S])
        par = sb("par", [P, NPAR])
        sw = sb("sw", [P, 8, P])
        cst = sb("cst", [P, NCONST])
        neg_half = sb("neg_half", [P, 2 * TT])
        stats = sb("stats", [P, TT, 4, 6])
        mv = sb("mv", [P, TT, 2])
        var_eps = sb("var_eps", [P, TT])
        rstd = sb("rstd", [P, TT])
        nmr = sb("nmr", [P, 1])
        ssq = sb("ssq", [P, 3, S])
        ms = sb("ms", [P, 3, TT])
        rms = sb("rms", [P, 3, TT])
        norm_eps = sb("norm_eps", [P, 1])
        pin = sb("pin", [P, 1])
        zf = feat[:, 16:20, :]
        uv = feat[:, 20:28, :].rearrange("p (h t) (c) -> p h t c", t=TT)
        sq = feat[:, 20:28, :]
        odd_part = feat[:, 20:22, :].rearrange("p a (b s) -> p (a b) s", b=2)
        W = S + 2 * PAD
        flat = feat[:, 28:44, :].rearrange("p a s -> p (a s)")
        ln_g, ln_b = flat[:, 0:D], flat[:, D:2 * D]
        zp = flat[:, 0:4 * W].rearrange("p (a w) -> p a w", a=4)
        win = [flat[:, (1 + i) * 4 * W:(2 + i) * 4 * W].rearrange("p (a w) -> p a w", a=4) for i in range(2)]
        last_g = [scratch[:, 4 * c:4 * c + 4, :].rearrange("p a s -> p (a s)") for c in range(2)]
        last_b = [conv[:, :, :].rearrange("p a s -> p (a s)"), padded[:, :, :].rearrange("p a s -> p (a s)")[:, 0:4 * S]]
        ident = cst[:, K_ID:K_ID + P]
        ones_pool = cst[:, K_ONE5:K_ONE5 + 1]
        ones_conv = cst[:, K_ONE10:K_ONE10 + 1]
        dft_c = cst[:, K_DFTC:K_DFTC + 2 * P]
        dft_s = cst[:, K_DFTS:K_DFTS + 2 * S].rearrange("p (t a s) -> p t a s", t=TT, a=2)
        inv_count = cst[:, K_INV:K_INV + 4 * S].rearrange("p (a s) -> p a s", a=4)
        ps = ctx.enter_context(nc.psum_tensor("ps", [P, 8, 512], F32))
        fr_halves = ps[:, 0:2, :].rearrange("p b (h r s) -> p (b h) r s", h=2, r=2)

        panel_landed = [sem(f"panel_landed{i}") for i in range(RING)]
        hi_cut = [sem(f"hi_cut{i}") for i in range(RING)]
        lo_cut = [sem(f"lo_cut{i}") for i in range(RING)]
        used = [sem(f"used{i}") for i in range(RING)]
        slots_seen = sem("slots_seen")
        tables_in = sem("tables_in")
        consts_in, params_in, ln_rows_in = sem("consts_in"), sem("params_in"), sem("ln_rows_in")
        small_w_in = sem("small_w_in")
        x_in = [sem(f"x_in{n}") for n in range(4 * TT)]
        eps_set = sem("eps_set")
        pads_zero, neg_half_set = sem("pads_zero"), sem("neg_half_set")
        y_added, stats_done, mv_done, var_ready = sem("y_added"), sem("stats_done"), sem("mv_done"), sem("var_ready")
        rstd_ready, nmr_ready = sem("rstd_ready"), sem("nmr_ready")
        norm0, norm1 = sem("norm0"), sem("norm1")
        transposed, xf_ready, xT_hi, xT_ready = sem("transposed"), sem("xf_ready"), sem("xT_hi"), sem("xT_ready")
        resid_scaled, resid_ready = sem("resid_scaled"), sem("resid_ready")
        low_copied = sem("low_copied")
        sums_out = sem("sums_out")
        bank_done = sem("bank_done")
        zp_ready, window, pooled = sem("zp_ready"), sem("window"), sem("pooled")
        uv_done, uv_act, uv_dve = sem("uv_done"), sem("uv_act"), sem("uv_dve")
        fr_done, fr_act, fr_dve = sem("fr_done"), sem("fr_act"), sem("fr_dve")
        proj_done, yb_ready, yc_ready = sem("proj_done"), sem("yb_ready"), sem("yc_ready")
        sq_step, ssq_pf = sem("sq_step"), sem("ssq_pf")
        ms_pf_done, ms_pf_ready, rms_pf = sem("ms_pf_done"), sem("ms_pf_ready"), sem("rms_pf")
        cv_ready, mid_ready, tap0 = sem("cv_ready"), sem("mid_ready"), sem("tap0")
        conv_done, ya_ready = sem("conv_done"), sem("ya_ready")
        sqa_step, ssq_a = sem("sqa_step"), sem("ssq_a")
        ms_a_done, ms_a_ready, rms_a = sem("ms_a_done"), sem("ms_a_ready"), sem("rms_a")
        g_mid, g_tap0, g_conv, gelu_done, h_ready = sem("g_mid"), sem("g_tap0"), sem("g_conv"), sem("gelu_done"), sem("h_ready")
        fin_a0, fin_b0 = sem("fin_a0"), sem("fin_b0")
        fin_a1, fin_b1 = sem("fin_a1"), sem("fin_b1")
        stored = sem("stored")
        last_rows_in = sem("last_rows_in")

        block = ctx.enter_context(nc.Block())

        def last_row(halves, c, w):
            return halves[c // 1024][:, c % 1024:c % 1024 + w]

        def lap(l, c, i=None, step=0):
            v = LAPS * l + c // RING + 1
            return v if i is None else v + step // RING * i

        def plap(l, c, i=None, step=0):
            v = PLAPS * l + c // 8 + 1
            return v if i is None else v + step // 8 * i

        def bank(s, b):
            return 4 * s + b

        def cut_out(eng, cut, l, chunk):
            k = (chunk - OUT_C) % KT
            if chunk - OUT_C == 0:
                eng.wait_ge(yb_ready, l + 1)
            if chunk - OUT_C == 4:
                eng.wait_ge(yc_ready, l + 1)
            if chunk - OUT_C == 8:
                eng.wait_ge(ya_ready, 4 * l + 4)
            cut(l, chunk, k=k, gain=par[:, Q_MIXG + k:Q_MIXG + k + 1])

        @block.sync
        def _(sp):
            def load(l, p, src, i=None, step=0):
                last_chunk = 2 * (p - RING) + 1
                v = LAPS * l + last_chunk // RING + 1 + CREDIT
                sp.wait_ge(lo_cut[last_chunk % RING], v if i is None else v + 2 * step // RING * i)
                sp.sem_inc(slots_seen, 1)
                a = src.shape[0] // P
                dst = raw[:, p % RING, :].rearrange("p (a n) -> p a n", a=a)
                sp.dma_start(dst, src.rearrange("(a p) n -> p a n", p=P)).then_inc(panel_landed[p % RING], 16)

            for n in range(4 * TT):
                tt, c = n // 4, 512 * (n % 4)
                sp.dma_start(resid[:, tt, c:c + 512], x[0, tt * P:tt * P + P, c:c + 512]).then_inc(x_in[n], 16)
            with sp.Fori(0, DEPTH) as l:
                wi, wo, wg, wu, wd = (w.rearrange("l k n -> (l k) n") for w in (w_in, w_out, w_gate, w_up, w_down))
                for g, col in enumerate(MIX_COLS):
                    for q in range(4):
                        load(l, 4 * g + q, wi[bass.ds(D * l + 512 * q, 512), col:col + 512])
                for half in range(2):
                    for p in range(KT // 2):
                        row = 2 * P * ((p + 4) % 8)
                        load(l, OUT_C // 2 + 8 * half + p,
                             wo[bass.ds(D * l + row, 2 * P), 1024 * half:1024 * half + 1024])
                with sp.Fori(0, N_PAIR) as i:
                    for u, w in enumerate((wg, wu)):
                        for q in range(4):
                            load(l, FFN_C // 2 + 4 * u + q,
                                 w[bass.ds(D * l + 512 * q, 512), bass.ds(512 * i, 512)], i, 8)
                for half in range(2):
                    first = DOWN_C // 2 + half * FT // 2
                    cols = slice(1024 * half, 1024 * half + 1024)
                    for p in range(2):
                        load(l, first + p, wd[bass.ds(D_FF * l + 2 * P * p, 2 * P), cols])
                    with sp.Fori(0, (FT // 2 - 2) // 4) as i:
                        for p in range(2, 6):
                            load(l, first + p, wd[bass.ds(D_FF * l + 8 * P * i + 2 * P * p, 2 * P), cols], i, 4)
            sp.wait_ge(h_ready, 2 * N_PAIR * DEPTH)
            for r, dst in enumerate((last_g, last_b)):
                n = 4 * DEPTH + r
                for c in range(2):
                    sp.dma_start(dst[c], ln_rows[n:n + 1, 1024 * c:1024 * c + 1024].to_broadcast([P, 1024])).then_inc(last_rows_in, 16)
            for pieces, done, i in ((LAST_POOL, fin_b0, 0), (LAST_POOL, fin_b0, 1), (LAST_DVE, fin_b1, 0),
                                    (LAST_POOL, fin_b0, 2), (LAST_DVE, fin_b1, 1), (LAST_DVE, fin_b1, 2)):
                tt, c, w = pieces[i]
                sp.wait_ge(done, i + 1)
                sp.dma_start(out[0, tt * P:tt * P + P, c:c + w], resid[:, tt, c:c + w]).then_inc(stored, 16)
            sp.wait_ge(stored, 16 * (len(LAST_DVE) + len(LAST_POOL)))

        @block.tensor
        def _(pe):
            def wait_chunk(l, c, i=None, step=0):
                pe.wait_ge(lo_cut[c % RING], lap(l, c, i, step) + CREDIT)

            def column_chunk(l, s, c0, c, i=None, step=0):
                wait_chunk(l, c0 + c, i, step)
                slot = c % RING
                for kk in range(2):
                    k = 2 * c + kk
                    for t in range(4):
                        w = slice(512 * kk + P * t, 512 * kk + P * t + P)
                        T.matmul(ps[:, bank(s, t), :], w_hi[:, slot, w], xT[:, k, :], start=(k == 0), stop=False)
                        last = T.matmul(ps[:, bank(s, t), 0:S], w_lo[:, slot, w], xT[:, k, 0:S],
                                        start=False, stop=(k == KT - 1))
                last.then_inc(used[slot], 1)

            def row_chunk(l, s, c, first, final, i=None, step=0):
                wait_chunk(l, c, i, step)
                slot = c % RING
                for cb in range(2):
                    for tt in range(TT):
                        o = ps[:, bank(s, 2 * tt + cb), :]
                        tok, col = slice(P * tt, P * tt + P), slice(512 * cb, 512 * cb + 512)
                        T.matmul(o, m_hi[:, slot, tok], w_hi[:, slot, col], start=first, stop=False)
                        T.matmul(o, m_hi[:, slot, tok], w_lo[:, slot, col], start=False, stop=False)
                        last = T.matmul(o, m_lo[:, slot, tok], w_hi[:, slot, col], start=False, stop=final)
                        if final and (cb, tt) != (1, 1):
                            last.then_inc(bank_done, 1)
                last.then_inc(used[slot], 1)

            def last_row_chunks(l, s, c0):
                first = [(0, 0), (0, 1), (1, 0), (0, 2), (1, 1), (0, 3), (1, 2), (1, 3)]
                for b, slot in first + [(b, slot) for b in (2, 3) for slot in range(RING)]:
                    tt, cb = b // 2, b % 2
                    o = ps[:, bank(s, b), :]
                    tok, col = slice(P * tt, P * tt + P), slice(512 * cb, 512 * cb + 512)
                    if b == 0:
                        wait_chunk(l, c0 + slot)
                    T.matmul(o, m_hi[:, slot, tok], w_hi[:, slot, col], start=False, stop=False)
                    T.matmul(o, m_hi[:, slot, tok], w_lo[:, slot, col], start=False, stop=False)
                    last = T.matmul(o, m_lo[:, slot, tok], w_hi[:, slot, col], start=False, stop=(slot == RING - 1))
                    if b == 3:
                        last.then_inc(used[slot], 1)
                    elif slot == RING - 1:
                        last.then_inc(bank_done, 1)

            def transposes(n, s, tt, q):
                pe.wait_ge((norm0, norm1)[tt], 4 * n + q + 1)
                if q >= 2:
                    pe.wait_ge(xf_ready, 16 * n + 4 * (q - 2) + 4)
                for kk in range(4):
                    o = ps[:, bank(s, 2 * (q % 2) + kk // 2), S * (kk % 2) + P * tt:S * (kk % 2) + P * tt + P]
                    k = 4 * q + kk
                    last = T.transpose(o, resid[:, tt, P * k:P * k + P], ident)
                    if tt == 1 and kk % 2:
                        last.then_inc(transposed, 1)

            def first_column_group(l, n, s, c0):
                for tt in range(TT):
                    for q in range(2):
                        transposes(n, 1 - s, tt, q)
                for c in range(8):
                    if c in (2, 4):
                        for tt in range(TT):
                            transposes(n, 1 - s, tt, 1 + c // 2)
                    pe.wait_ge(xT_ready, 8 * n + c + 1)
                    column_chunk(l, s, c0, c)

            pe.wait_ge(consts_in, 16)
            for slot in range(RING):
                pe.sem_inc(used[slot], CREDIT)
            with pe.Fori(0, DEPTH) as l:
                first_column_group(l, 2 * l, 1, 0)
                for g in range(1, N_MIX):
                    s = (g + 1) % 2
                    if g in (5, 6, 7):
                        pe.wait_ge(sums_out, 2 * N_COLG * l + 2 * (g - 2) + 2)
                    if g == 2:
                        pe.wait_ge(uv_act, l + 1)
                        pe.wait_ge(uv_dve, l + 1)
                    if g == 3:
                        pe.wait_ge(fr_act, l + 1)
                        pe.wait_ge(fr_dve, l + 1)
                    if g == 4:
                        pe.wait_ge(yb_ready, l + 1)
                        pe.wait_ge(yc_ready, l + 1)
                    if g == 5:
                        pe.wait_ge(ms_pf_ready, l + 1)
                    for c in range(8):
                        if c == 4 and g == 1:
                            pe.wait_ge(tables_in, 16)
                            pe.wait_ge(sums_out, 2 * N_COLG * l + 2)
                            for h in range(4):
                                for tt in range(TT):
                                    last = T.matmul(ps[:, 4 + h, S * tt:S * tt + S], zf[:, h, tt:S:2],
                                                    dft_c, start=True, stop=True)
                            last.then_inc(uv_done, 1)
                        if c == 4 and g == 2:
                            pe.wait_ge(uv_act, l + 1)
                            pe.wait_ge(uv_dve, l + 1)
                            pe.wait_ge(sums_out, 2 * N_COLG * l + 4)
                            for h in range(4):
                                for parity in range(2):
                                    for part in range(2):
                                        col = S * (h % 2) + P * parity
                                        last = T.matmul(ps[:, h // 2, col:col + P], uv[:, h, parity, P * part:P * part + P],
                                                        dft_s[:, parity, part, :], start=(part == 0), stop=(part == 1))
                            last.then_inc(fr_done, 1)
                        if c == 4 and g == 3:
                            pe.wait_ge(fr_act, l + 1)
                            pe.wait_ge(fr_dve, l + 1)
                            pe.wait_ge(pooled, l + 1)
                            pe.wait_ge(small_w_in, 16 * l + 16)
                            pe.wait_ge(sums_out, 2 * N_COLG * l + 6)
                            for h in range(8):
                                rhs = zf[:, h, :] if h < 4 else zp[:, h - 4, PAD:PAD + S]
                                last = T.matmul(ps[:, 4 + h // 2, S * (h % 2):S * (h % 2) + S], sw[:, h, :], rhs,
                                                start=True, stop=True)
                            last.then_inc(proj_done, 1)
                        if c == 4 and g == 4:
                            pe.wait_ge(ssq_pf, l + 1)
                            pe.wait_ge(sums_out, 2 * N_COLG * l + 8)
                            for r in range(2):
                                for tt in range(TT):
                                    last = T.matmul(ps[:, 0, 2 * r + tt:2 * r + tt + 1], ssq[:, r, P * tt:P * tt + P],
                                                    ones_pool, start=True, stop=True)
                            last.then_inc(ms_pf_done, 1)
                        column_chunk(l, s, 8 * g, c)
                for r in range(6):
                    s, (k0, kn, _) = 1 - r % 2, OUT_PARTS[r % 3]
                    base = OUT_C + KT * (r // 3) + k0
                    if r < 2:
                        pe.wait_ge(sums_out, 2 * N_COLG * l + 2 * (6 + r) + 2)
                    else:
                        pe.wait_ge(y_added, 32 * l + 4 * (r - 2) + 4)
                    if r == 2:
                        pe.wait_ge(ms_a_ready, l + 1)
                    for c in range(kn - RING if r == 5 else kn):
                        if r == 1 and c == 3:
                            pe.wait_ge(ssq_a, 2 * l + 2)
                            pe.wait_ge(y_added, 32 * l + 4)
                            for tt in range(TT):
                                last = T.matmul(ps[:, 4, tt:tt + 1], ssq[:, 2, P * tt:P * tt + P], ones_conv,
                                                start=True, stop=True)
                            last.then_inc(ms_a_done, 1)
                        row_chunk(l, s, base + c, c == 0, c == kn - 1)
                last_row_chunks(l, 0, FFN_C - RING)
                first_column_group(l, 2 * l + 1, 0, FFN_C)
                pe.wait_ge(xf_ready, 16 * (2 * l + 1) + 16)
                for c in range(8):
                    column_chunk(l, 1, FFN_C + 8, c)
                with pe.Fori(0, N_PAIR - 1) as i:
                    for u in range(2):
                        pe.wait_ge(sums_out, 2 * N_COLG * l + 2 * (N_MIX + u) + 2 + 4 * i)
                        for c in range(8):
                            column_chunk(l, u, FFN_C + 16 + 8 * u, c, i, 16)
                for half in range(2):
                    base = DOWN_C + FT * half
                    pe.wait_ge(sums_out, 2 * N_COLG * l + 2 * (N_COLG - 2 + half) + 2)
                    for c in range(4):
                        row_chunk(l, half, base + c, c == 0, False)
                    with pe.Fori(0, FT // 4 - 2) as i:
                        for c in range(4):
                            row_chunk(l, half, base + 4 + c, False, False, i, 4)
                    if half == 0:
                        for c in range(FT - 4, FT):
                            row_chunk(l, half, base + c, False, c == FT - 1)
                    else:
                        last_row_chunks(l, half, base + FT - RING)

        @block.scalar
        def _(act):
            def cut_hi(l, c, i=None, step=0, k=None, gain=1.0):
                slot = c % RING
                act.wait_ge(used[slot], lap(l, c, i, step) - 1 + CREDIT)
                if k is not None:
                    A.activation(m_hi[:, slot, :], feat[:, k, :], ACT.Copy, scale=gain)
                act.wait_ge(panel_landed[c // 2 % RING], 16 * plap(l, c, i, step))
                A.activation(w_hi[:, slot, :], raw[:, c // 2 % RING, 1024 * (c % 2):1024 * (c % 2) + 1024],
                             ACT.Copy).then_inc(hi_cut[slot], 1)

            def copy_low(l, g, st, c_last, i=None, pair=0):
                s = (g + 1) % 2 if g < N_MIX else (g - N_MIX) % 2
                if st == 0:
                    act.wait_ge(used[3], lap(l, c_last, i, 16 if i is not None else 0) + CREDIT)
                A.activation(low[:, 2 * st:2 * st + 2, :], ps[:, bank(s, 2 * st):bank(s, 2 * st) + 2, S:2 * S],
                             ACT.Copy).then_inc(low_copied, 1)

            def centre_tap(tile, w, b, done):
                A.activation(mid[:, tile, :], padded[:, tile, 1:S + 1], ACT.Identity, bias=b, scale=w).then_inc(done, 1)

            def norm_rows(q):
                A.activation(resid[:, 0, 512 * q:512 * q + 512], resid[:, 0, 512 * q:512 * q + 512], ACT.Identity,
                             bias=nmr[:, 0:1], scale=rstd[:, 0:1]).then_inc(norm0, 1)

            def read_transposed(n, s, q, qg, qb):
                if q >= 2:
                    act.wait_ge(xT_ready, 8 * n + 2 * (q - 2) + 2)
                for kk in range(4):
                    k = 4 * q + kk
                    if kk % 2 == 0:
                        act.wait_ge(transposed, 8 * n + k // 2 + 1)
                    A.activation(xf[:, q % 2, kk, :], ps[:, bank(s, 2 * (q % 2) + kk // 2), S * (kk % 2):S * (kk % 2) + S],
                                 ACT.Identity, bias=par[:, qb + k:qb + k + 1],
                                 scale=par[:, qg + k:qg + k + 1]).then_inc(xf_ready, 1)

            def behind_norm(l, n, s, c0, qg, qb):
                act.wait_ge(nmr_ready, n + 1)
                norm_rows(0)
                norm_rows(1)
                cut_hi(l, c0)
                cut_hi(l, c0 + 1)
                act.wait_ge(params_in, 16 * l + 16)
                read_transposed(n, 1 - s, 0, qg, qb)
                cut_hi(l, c0 + 2)
                read_transposed(n, 1 - s, 1, qg, qb)
                norm_rows(2)
                norm_rows(3)
                for c in range(8):
                    cut_hi(l, c0 + c + AHEAD)
                    if c in (2, 4):
                        read_transposed(n, 1 - s, 1 + c // 2, qg, qb)
                    if c == 5 and s == 1:
                        act.dma_start(sw[:, :, :].rearrange("p a n -> p (a n)"),
                                      small_w[bass.ds(P * l, P), :]).then_inc(small_w_in, 16)
                        for r, dst in enumerate((ln_g, ln_b)):
                            act.dma_start(dst, ln_rows[bass.ds(4 * l + r, 1), :].to_broadcast([P, D])).then_inc(ln_rows_in, 16)

            def gate_hooks(c, l, i, c_last, tile0):
                n_before = 4 * N_PAIR * l + 4 * i if i is not None else 4 * N_PAIR * l + 4 * (N_PAIR - 1)
                g = N_MIX
                if c in (0, 1):
                    copy_low(l, g, c, c_last, i)
                if c in (1, 2):
                    v = 2 * N_COLG * l + 2 * N_MIX
                    v = v + 4 * i if i is not None else v + 4 * (N_PAIR - 1)
                    act.wait_ge(sums_out, v + c)
                    for t in (2 * c - 2, 2 * c - 1):
                        centre_tap(t, par[:, fcol(Q_FCW + FT, tile0, t)], par[:, fcol(Q_FCB, tile0, t)], g_mid)
                if c in (3, 4):
                    if c == 3:
                        act.wait_ge(resid_ready, 2 * l + 2)
                    for t in (2 * c - 6, 2 * c - 5):
                        act.wait_ge(g_conv, n_before + t + 1)
                        A.activation(feat[:, fcol(0, tile0, t), :], conv[:, t:t + 1, :], ACT.Gelu).then_inc(gelu_done, 1)

            def fcol(base, tile0, t):
                return bass.ds(tile0 + (base + t), 1)

            act.dma_start(cst[:, 0:K_DFTC], consts[:, 0:K_DFTC]).then_inc(consts_in, 16)

            with act.Fori(0, DEPTH) as l:
                act.dma_start(par[:, :], params[bass.ds(P * l, P), :]).then_inc(params_in, 16)
                behind_norm(l, 2 * l, 1, 0, Q_LNA_G, Q_LNA_B)
                for g in range(1, N_MIX + 1):
                    for c in range(8):
                        chunk = 8 * g + c + AHEAD
                        if g == N_MIX:
                            break
                        if chunk >= OUT_C:
                            cut_out(act, cut_hi, l, chunk)
                        else:
                            cut_hi(l, chunk)
                        if c in (0, 1):
                            copy_low(l, g - 1, c, 8 * g - 1)
                        if g in (4, 7) and c in (2, 3):
                            act.wait_ge(cv_ready, 4 * l + 2 * (g // 6) + c - 1)
                            for t in (2 * c - 4, 2 * c - 3):
                                q = Q_CONV + CONV_TILES + 4 * (g // 6) + t
                                centre_tap(t, par[:, q:q + 1], 0.0, mid_ready)
                        if c == 4 and g == 1:
                            act.wait_ge(uv_done, l + 1)
                            A.activation(uv[:, 0:2, :, :].rearrange("p h t c -> p h (t c)"), ps[:, 4:6, :], ACT.Copy).then_inc(uv_act, 1)
                        if c == 4 and g == 2:
                            act.wait_ge(fr_done, l + 1)
                            A.activation(odd_part, fr_halves[:, :, 1, :], ACT.Copy).then_inc(fr_act, 1)
                        if c == 4 and g == 3:
                            act.wait_ge(proj_done, l + 1)
                            for t in range(4):
                                last = A.activation(feat[:, t, :], ps[:, 6 + t // 2, S * (t % 2):S * (t % 2) + S], ACT.Copy,
                                                    scale=par[:, Q_PSC + t:Q_PSC + t + 1])
                            last.then_inc(yb_ready, 1)
                        if c == 4 and g == 5:
                            act.wait_ge(resid_ready, 2 * l + 1)
                            for r, dst in enumerate((ln_g, ln_b)):
                                act.dma_start(dst, ln_rows[bass.ds(2 * (2 * l + 1) + r, 1), :].to_broadcast([P, D])).then_inc(ln_rows_in, 16)
                for c in range(2 * KT):
                    if c + AHEAD < 2 * KT:
                        cut_out(act, cut_hi, l, OUT_C + c + AHEAD)
                    if c in (0, 1):
                        copy_low(l, N_MIX - 1, c, OUT_C - 1)
                behind_norm(l, 2 * l + 1, 0, FFN_C, Q_LN1_G, Q_LN1_B)
                with act.Fori(0, N_PAIR - 1) as i:
                    for c in range(8):
                        cut_hi(l, FFN_C + 8 + c + AHEAD, i, 16)
                        gate_hooks(c, l, i, FFN_C + 7, 4 * i)
                    for c in range(8):
                        cut_hi(l, FFN_C + 16 + c + AHEAD, i, 16)
                        if c in (0, 1):
                            copy_low(l, N_MIX + 1, c, FFN_C + 15, i)
                for c in range(8):
                    chunk = DOWN_C - 8 + c + AHEAD
                    if chunk >= DOWN_C:
                        cut_hi(l, chunk, k=chunk - DOWN_C)
                    else:
                        cut_hi(l, chunk)
                    gate_hooks(c, l, None, DOWN_C - 9, 4 * (N_PAIR - 1))
                for half in range(2):
                    base = DOWN_C + FT * half
                    for c in range(8):
                        if half == 0 and c == 2:
                            act.wait_ge(h_ready, 2 * N_PAIR * l + 2 * N_PAIR)
                        cut_hi(l, base + c + AHEAD, k=c + AHEAD)
                        if half == 0 and c in (0, 1):
                            copy_low(l, N_COLG - 1, c, DOWN_C - 1)
                    with act.Fori(0, FT // 8 - 1) as i:
                        for c in range(8):
                            cut_hi(l, base + 8 + c + AHEAD, i, 8, k=bass.ds(8 * i + (8 + c + AHEAD), 1))
                    for c in range(FT - 4, FT):
                        if c + AHEAD < FT or half == 0:
                            cut_hi(l, base + c + AHEAD, k=(c + AHEAD) % FT)
            act.wait_ge(nmr_ready, 2 * DEPTH + 1)
            for q in range(3):
                norm_rows(q)

        @block.vector
        def _(dve):
            def cut_lo(l, c, i=None, step=0, k=None, gain=None):
                slot = c % RING
                dve.wait_ge(hi_cut[slot], lap(l, c, i, step))
                if gain is not None:
                    V.scalar_tensor_tensor(out=m_lo[:, slot, :], in0=feat[:, k, :], scalar=gain,
                                           in1=m_hi[:, slot, :].bitcast(F32), op0=ALU.mult, op1=ALU.subtract)
                elif k is not None:
                    V.tensor_tensor(m_lo[:, slot, :], feat[:, k, :], m_hi[:, slot, :].bitcast(F32), ALU.subtract)
                V.tensor_tensor(w_lo[:, slot, :], raw[:, c // 2 % RING, 1024 * (c % 2):1024 * (c % 2) + 1024],
                                w_hi[:, slot, :].bitcast(F32), ALU.subtract).then_inc(lo_cut[slot], 1)

            def add_halves(l, g, st, dst, i=None):
                s = (g + 1) % 2 if g < N_MIX else (g - N_MIX) % 2
                v = 2 * N_COLG * l + 2 * g + st + 1
                dve.wait_ge(low_copied, v if i is None else v + 4 * i)
                V.tensor_tensor(dst, ps[:, bank(s, 2 * st):bank(s, 2 * st) + 2, 0:S], low[:, 2 * st:2 * st + 2, :],
                                ALU.add).then_inc(sums_out, 1)

            def after_sum(l, g, st, i=None):
                v = 2 * N_COLG * l + 2 * g + st + 1
                dve.wait_ge(sums_out, v if i is None else v + 4 * i)

            def add_row_bank(l, r, s, j):
                tt, cb = (j // 2, j % 2) if r in (5, 7) else (j % 2, j // 2)
                if j < 3:
                    dve.wait_ge(bank_done, 24 * l + 3 * r + j + 1)
                else:
                    last_chunk = (OUT_C + KT * (r // 3) + sum(OUT_PARTS[r % 3][:2]) if r < 6 else DOWN_C + FT * (r - 5)) - 1
                    dve.wait_ge(used[3], lap(l, last_chunk) + CREDIT)
                half = r // 3 if r < 6 else r - 6
                y = resid[:, tt, 1024 * half + 512 * cb:1024 * half + 512 * cb + 512]
                factor = rms[:, r % 3, tt:tt + 1] if r < 6 else 1.0 / ALPHA
                if r < 6 and r % 3:
                    dve.wait_ge(y_added, 32 * l + 4 * (r - 1) + 4)
                V.scalar_tensor_tensor(out=y, in0=ps[:, bank(s, 2 * tt + cb), :], scalar=factor, in1=y,
                                       op0=ALU.mult, op1=ALU.add).then_inc(y_added, 1)
                if r in (2, 5, 6, 7):
                    dve.wait_ge(y_added, 32 * l + 4 * r + j + 1)
                    V.bn_stats(stats[:, tt, 2 * half + cb, :], y).then_inc(stats_done, 1)

            def mean_var(n, tt, n_stats):
                dve.wait_ge(stats_done, 8 * n + n_stats)
                V.memset(pin[:, :], 0.0)
                V.bn_aggr(mv[:, tt, :], stats[:, tt, :, :].rearrange("p a b -> p (a b)")).then_inc(mv_done, 1)
                dve.wait_ge(mv_done, TT * n + tt + 1)
                V.tensor_scalar(var_eps[:, tt:tt + 1], mv[:, tt, 1:2], norm_eps[:, 0:1], None, ALU.add).then_inc(var_ready, 1)

            def scale_rows0(n):
                dve.wait_ge(rstd_ready, TT * n + 1)
                V.scalar_tensor_tensor(out=nmr[:, :], in0=mv[:, 0, 0:1], scalar=-1.0, in1=rstd[:, 0:1],
                                       op0=ALU.mult, op1=ALU.mult).then_inc(nmr_ready, 1)

            def last_sums(l, r, s, n):
                for j in range(4):
                    if j == 2:
                        mean_var(n, 0, 6)
                        scale_rows0(n)
                    add_row_bank(l, r, s, j)

            def cut_x(n, p):
                q, kk = p // 2, 2 * (p % 2)
                src = xf[:, q % 2, kk:kk + 2, :]
                dve.wait_ge(xf_ready, 16 * n + 2 * p + 2)
                V.tensor_copy(xT[:, 2 * p:2 * p + 2, 0:S], src).then_inc(xT_hi, 1)
                dve.wait_ge(xT_hi, 8 * n + p + 1)
                V.tensor_tensor(xT[:, 2 * p:2 * p + 2, S:2 * S], src, xT[:, 2 * p:2 * p + 2, 0:S].bitcast(F32),
                                ALU.subtract).then_inc(xT_ready, 1)

            def behind_norm(l, n, c0):
                def norm_rows(q):
                    y = resid[:, 1, 512 * q:512 * q + 512]
                    V.tensor_scalar(y, y, mv[:, 1, 0:1], rstd[:, 1:2], ALU.subtract, ALU.mult).then_inc(norm1, 1)

                mean_var(n, 1, 8)
                dve.wait_ge(rstd_ready, TT * n + 2)
                norm_rows(0)
                norm_rows(1)
                cut_lo(l, c0)
                cut_x(n, 0)
                cut_x(n, 1)
                cut_lo(l, c0 + 1)
                norm_rows(2)
                norm_rows(3)
                cut_x(n, 2)
                cut_x(n, 3)
                cut_lo(l, c0 + 2)
                for c in range(8):
                    cut_lo(l, c0 + c + AHEAD)
                    if c in (2, 4):
                        cut_x(n, 2 + c)
                        cut_x(n, 3 + c)

            def outer_taps(t, w0, w2, mid_sem, n_mid, tap_sem, n_tap, done):
                for u in (t, t + 1):
                    dve.wait_ge(mid_sem, n_mid + u + 1)
                    V.scalar_tensor_tensor(out=conv[:, u, :], in0=padded[:, u, 0:S], scalar=w0(u), in1=mid[:, u, :],
                                           op0=ALU.mult, op1=ALU.add).then_inc(tap_sem, 1)
                for u in (t, t + 1):
                    dve.wait_ge(tap_sem, n_tap + u + 1)
                    V.scalar_tensor_tensor(out=conv[:, u, :], in0=padded[:, u, 2:S + 2], scalar=w2(u), in1=conv[:, u, :],
                                           op0=ALU.mult, op1=ALU.add).then_inc(done, 1)

            def gate_hooks(c, l, i, g, tile0):
                if c in (0, 1):
                    add_halves(l, g, c, padded[:, 2 * c:2 * c + 2, 1:S + 1], i)
                if c in (2, 3):
                    n = 4 * N_PAIR * l + (4 * i if i is not None else 4 * (N_PAIR - 1))
                    outer_taps(2 * c - 4, lambda u: par[:, bass.ds(tile0 + (Q_FCW + u), 1)],
                               lambda u: par[:, bass.ds(tile0 + (Q_FCW + 2 * FT + u), 1)], g_mid, n, g_tap0, n, g_conv)

            def up_hooks(c, l, i, g, tile0):
                if c in (0, 1):
                    add_halves(l, g, c, conv[:, 2 * c:2 * c + 2, :], i)
                    after_sum(l, g, c, i)
                    h = feat[:, bass.ds(tile0 + 2 * c, 2), :]
                    V.tensor_tensor(h, h, conv[:, 2 * c:2 * c + 2, :], ALU.mult).then_inc(h_ready, 1)

            def conv_output(l, grp, g, st):
                t = 8 + 4 * grp + 2 * st
                add_halves(l, g, st, feat[:, t:t + 2, :])
                after_sum(l, g, st)
                V.tensor_tensor(feat[:, t:t + 2, :], feat[:, t:t + 2, :], conv[:, 2 * st:2 * st + 2, :],
                                ALU.mult).then_inc(ya_ready, 1)

            for slot in range(RING):
                dve.sem_inc(lo_cut[slot], CREDIT)
            V.memset(norm_eps[:, :], LN_EPS).then_inc(eps_set, 1)
            V.memset(neg_half[:, :], -0.5).then_inc(neg_half_set, 1)
            V.memset(padded[:, :, :], 0.0).then_inc(pads_zero, 1)
            for tt in range(TT):
                for q in range(4):
                    dve.wait_ge(x_in[4 * tt + q], 16)
                    V.bn_stats(stats[:, tt, q, :], resid[:, tt, 512 * q:512 * q + 512]).then_inc(stats_done, 1)
                if tt == 0:
                    dve.wait_ge(eps_set, 1)
                    mean_var(0, 0, 4)
            scale_rows0(0)
            dve.wait_ge(pads_zero, 1)
            with dve.Fori(0, DEPTH) as l:
                dve.wait_ge(eps_set, l + 1)
                behind_norm(l, 2 * l, 0)
                V.memset(norm_eps[:, :], LN_EPS / ALPHA ** 2).then_inc(eps_set, 1)
                dve.wait_ge(params_in, 16 * l + 16)
                for g in range(1, N_MIX):
                    for c in range(8):
                        chunk = 8 * g + c + AHEAD
                        if chunk >= OUT_C:
                            cut_out(dve, cut_lo, l, chunk)
                        else:
                            cut_lo(l, chunk)
                        two = slice(2 * c, 2 * c + 2)
                        if c in (0, 1):
                            if g == 1:
                                add_halves(l, 0, c, zf[:, two, :])
                            if g == 2:
                                if c == 0:
                                    dve.wait_ge(resid_ready, 2 * l + 1)
                                    V.memset(zp[:, :, 0:PAD], 0.0)
                                    V.memset(zp[:, :, PAD + S:W], 0.0)
                                add_halves(l, 1, c, zp[:, two, PAD:PAD + S])
                            if g in (3, 6):
                                add_halves(l, g - 1, c, conv[:, two, :])
                            if g in (4, 7):
                                add_halves(l, g - 1, c, padded[:, two, 1:S + 1])
                                after_sum(l, g - 1, c)
                                V.tensor_tensor(padded[:, two, 1:S + 1], padded[:, two, 1:S + 1], conv[:, two, :],
                                                ALU.mult).then_inc(cv_ready, 1)
                            if g == 5:
                                conv_output(l, 0, 4, c)
                        if g in (4, 7) and c in (3, 4):
                            grp = g // 6
                            q = Q_CONV + 4 * grp
                            n = 8 * l + 4 * grp
                            outer_taps(2 * c - 6, lambda u: par[:, q + u:q + u + 1],
                                       lambda u: par[:, q + 2 * CONV_TILES + u:q + 2 * CONV_TILES + u + 1],
                                       mid_ready, n, tap0, n, conv_done)
                        if c == 4 and g == 1:
                            dve.wait_ge(uv_done, l + 1)
                            V.tensor_copy(uv[:, 2:4, :, :].rearrange("p h t c -> p h (t c)"), ps[:, 6:8, :]).then_inc(uv_dve, 1)
                        if c == 4 and g == 2:
                            dve.wait_ge(fr_act, l + 1)
                            V.tensor_tensor(zf[:, :, 0:P], fr_halves[:, :, 0, :], odd_part, ALU.add)
                            V.tensor_tensor(zf[:, :, P:S], fr_halves[:, :, 0, :], odd_part, ALU.subtract).then_inc(fr_dve, 1)
                        if c == 4 and g == 3:
                            dve.wait_ge(proj_done, l + 1)
                            V.tensor_copy(feat[:, 4:8, :], ps[:, 4:6, :].rearrange("p b (a s) -> p (b a) s", a=2)).then_inc(yc_ready, 1)
                        if c == 5 and g == 4:
                            dve.wait_ge(ms_pf_done, l + 1)
                            V.tensor_scalar(ms[:, 0:2, :], ps[:, 0, 0:2 * TT].rearrange("p (a t) -> p a t", a=2), RMS_EPS,
                                            ALPHA * ALPHA, ALU.add, ALU.mult).then_inc(ms_pf_ready, 1)
                for c in range(2 * KT):
                    if c == 7:
                        dve.wait_ge(ms_a_done, l + 1)
                        V.tensor_scalar(ms[:, 2, :], ps[:, 4, 0:TT], RMS_EPS, ALPHA * ALPHA, ALU.add,
                                        ALU.mult).then_inc(ms_a_ready, 1)
                    if c + AHEAD < 2 * KT:
                        cut_out(dve, cut_lo, l, OUT_C + c + AHEAD)
                    if c in (0, 1):
                        conv_output(l, 1, N_MIX - 1, c)
                    for r in range(5):
                        first = KT * ((r + 1) // 3) + OUT_PARTS[(r + 1) % 3][0]
                        if c in (first, first + 1):
                            if c == first and r == 0:
                                dve.wait_ge(rms_pf, l + 1)
                            if c == first and r == 2:
                                dve.wait_ge(rms_a, l + 1)
                            for j in (2 * (c - first), 2 * (c - first) + 1):
                                add_row_bank(l, r, 1 - r % 2, j)
                dve.wait_ge(eps_set, l + 2)
                last_sums(l, 5, 0, 2 * l + 1)
                behind_norm(l, 2 * l + 1, FFN_C)
                with dve.Fori(0, N_PAIR - 1) as i:
                    for c in range(8):
                        cut_lo(l, FFN_C + 8 + c + AHEAD, i, 16)
                        gate_hooks(c, l, i, N_MIX, 4 * i)
                    for c in range(8):
                        cut_lo(l, FFN_C + 16 + c + AHEAD, i, 16)
                        up_hooks(c, l, i, N_MIX + 1, 4 * i)
                for c in range(8):
                    chunk = DOWN_C - 8 + c + AHEAD
                    if chunk >= DOWN_C:
                        if chunk == DOWN_C:
                            dve.wait_ge(h_ready, 2 * N_PAIR * l + 2 * N_PAIR - 2)
                        cut_lo(l, chunk, k=chunk - DOWN_C)
                    else:
                        cut_lo(l, chunk)
                    gate_hooks(c, l, None, N_COLG - 2, 4 * (N_PAIR - 1))
                for half in range(2):
                    base = DOWN_C + FT * half
                    for c in range(8):
                        if half == 0 and c == 2:
                            dve.wait_ge(h_ready, 2 * N_PAIR * l + 2 * N_PAIR)
                        cut_lo(l, base + c + AHEAD, k=c + AHEAD)
                        if half == 0:
                            up_hooks(c, l, None, N_COLG - 1, 4 * (N_PAIR - 1))
                        elif c in (0, 1):
                            for j in (2 * c, 2 * c + 1):
                                add_row_bank(l, 6, 0, j)
                    with dve.Fori(0, FT // 8 - 1) as i:
                        for c in range(8):
                            cut_lo(l, base + 8 + c + AHEAD, i, 8, k=bass.ds(8 * i + (8 + c + AHEAD), 1))
                    for c in range(FT - 4, FT):
                        if c + AHEAD < FT or half == 0:
                            cut_lo(l, base + c + AHEAD, k=(c + AHEAD) % FT)
                last_sums(l, 7, 1, 2 * l + 2)
            n = 2 * DEPTH
            mean_var(n, 1, 8)
            dve.wait_ge(last_rows_in, 64)
            for i, (tt, c, w) in enumerate(LAST_DVE):
                y = resid[:, tt, c:c + w]
                V.scalar_tensor_tensor(out=y, in0=y, scalar=mv[:, tt, 0:1], in1=last_row(last_g, c, w),
                                       op0=ALU.subtract, op1=ALU.mult).then_inc(fin_a1, 1)
                dve.wait_ge(fin_a1, i + 1)
                if i == 0:
                    dve.wait_ge(rstd_ready, TT * n + 2)
                V.scalar_tensor_tensor(out=y, in0=y, scalar=rstd[:, tt:tt + 1], in1=last_row(last_b, c, w),
                                       op0=ALU.mult, op1=ALU.add).then_inc(fin_b1, 1)

        @block.gpsimd
        def _(pool):
            def power(src, dst, width, ready, n, done):
                pool.wait_ge(ready, n)
                G.tensor_tensor(dst, src, neg_half[:, 0:width], ALU.pow).then_inc(done, 1)

            def row_rstd(n, tt):
                power(var_eps[:, tt:tt + 1], rstd[:, tt:tt + 1], 1, var_ready, TT * n + tt + 1, rstd_ready)

            def make_residual(n):
                pool.wait_ge(ln_rows_in, 32 * n + 32)
                pool.wait_ge(transposed, 8 * n + 8)
                for tt in range(TT):
                    G.tensor_tensor(resid[:, tt, :], resid[:, tt, :], ln_g, ALU.mult).then_inc(resid_scaled, 1)
                for tt in range(TT):
                    pool.wait_ge(resid_scaled, 2 * n + tt + 1)
                    last = G.tensor_tensor(resid[:, tt, :], resid[:, tt, :], ln_b, ALU.add)
                last.then_inc(resid_ready, 1)

            pool.wait_ge(neg_half_set, 1)
            row_rstd(0, 0)
            pool.dma_start(cst[:, K_DFTC:NCONST], consts[:, K_DFTC:NCONST]).then_inc(tables_in, 16)
            with pool.Fori(0, DEPTH) as l:
                row_rstd(2 * l, 1)
                make_residual(2 * l)
                pool.wait_ge(sums_out, 2 * N_COLG * l + 4)
                src, lo_edge, hi_edge = zp, 0, W
                for lev, half in enumerate(POOL_HALF):
                    sh = max(half // 2, 0)
                    dst = win[lev % 2]
                    if lev == 0:
                        lo_edge = 1
                        a, b = zp[:, :, 0:W - 1], zp[:, :, 1:W]
                        o = dst[:, :, 1:W]
                    else:
                        lo_edge, hi_edge = lo_edge + sh, hi_edge - sh
                        a = src[:, lev:4, lo_edge - sh:hi_edge - sh]
                        b = src[:, lev:4, lo_edge + sh:hi_edge + sh]
                        o = dst[:, lev:4, lo_edge:hi_edge]
                        pool.wait_ge(window, 9 * l + lev)
                    G.tensor_tensor(o, a, b, ALU.add).then_inc(window, 1)
                    src = dst
                pool.wait_ge(window, 9 * l + 4)
                pool.wait_ge(tables_in, 16)
                for g in range(4):
                    o = win[g % 2][:, g, PAD:PAD + S]
                    G.tensor_tensor(o, o, inv_count[:, g, :], ALU.mult).then_inc(window, 1)
                for g in range(4):
                    pool.wait_ge(window, 9 * l + 5 + g)
                    last = G.tensor_tensor(zp[:, g, PAD:PAD + S], win[g % 2][:, g, PAD:PAD + S], zp[:, g, PAD:PAD + S],
                                           ALU.subtract)
                    if g == 0:
                        last.then_inc(window, 1)
                last.then_inc(pooled, 1)
                pool.wait_ge(yb_ready, l + 1)
                pool.wait_ge(yc_ready, l + 1)
                G.tensor_tensor(sq[:, :, :], feat[:, 0:8, :], feat[:, 0:8, :], ALU.mult).then_inc(sq_step, 1)
                sqv = sq.rearrange("p (g t) s -> p g t s", g=2)
                pool.wait_ge(sq_step, 2 * l + 1)
                G.tensor_tensor(sqv[:, :, 0:2, :], sqv[:, :, 0:2, :], sqv[:, :, 2:4, :], ALU.add).then_inc(sq_step, 1)
                pool.wait_ge(sq_step, 2 * l + 2)
                G.tensor_tensor(ssq[:, 0:2, :], sqv[:, :, 0, :], sqv[:, :, 1, :], ALU.add).then_inc(ssq_pf, 1)
                power(ms[:, 0:2, :].rearrange("p a t -> p (a t)"), rms[:, 0:2, :].rearrange("p a t -> p (a t)"), 2 * TT,
                      ms_pf_ready, l + 1, rms_pf)
                pool.wait_ge(ssq_pf, l + 1)
                for h in range(2):
                    y = feat[:, 8 + 4 * h:12 + 4 * h, :]
                    pool.wait_ge(ya_ready, 4 * l + 2 * h + 2)
                    G.tensor_tensor(sq[:, 0:4, :], y, y, ALU.mult).then_inc(sqa_step, 1)
                    pool.wait_ge(sqa_step, 5 * l + 2 * h + 1)
                    G.tensor_tensor(sq[:, 0:2, :], sq[:, 0:2, :], sq[:, 2:4, :], ALU.add).then_inc(sqa_step, 1)
                    pool.wait_ge(sqa_step, 5 * l + 2 * h + 2)
                    if h == 0:
                        G.tensor_tensor(ssq[:, 2, :], sq[:, 0, :], sq[:, 1, :], ALU.add).then_inc(ssq_a, 1)
                        pool.wait_ge(ssq_a, 2 * l + 1)
                    else:
                        G.tensor_tensor(sq[:, 0, :], sq[:, 0, :], sq[:, 1, :], ALU.add).then_inc(sqa_step, 1)
                        pool.wait_ge(sqa_step, 5 * l + 5)
                        G.tensor_tensor(ssq[:, 2, :], ssq[:, 2, :], sq[:, 0, :], ALU.add).then_inc(ssq_a, 1)
                power(ms[:, 2, :], rms[:, 2, :], TT, ms_a_ready, l + 1, rms_a)
                row_rstd(2 * l + 1, 0)
                row_rstd(2 * l + 1, 1)
                make_residual(2 * l + 1)
                row_rstd(2 * l + 2, 0)
            n = 2 * DEPTH
            pool.wait_ge(last_rows_in, 64)
            for i, (tt, c, w) in enumerate(LAST_POOL):
                y = resid[:, tt, c:c + w]
                pool.wait_ge(norm0, 4 * n + (c + w) // 512)
                G.tensor_tensor(y, y, last_row(last_g, c, w), ALU.mult).then_inc(fin_a0, 1)
                if i == 1:
                    row_rstd(n, 1)
                pool.wait_ge(fin_a0, i + 1)
                G.tensor_tensor(y, y, last_row(last_b, c, w), ALU.add).then_inc(fin_b0, 1)


def kernel(**inputs):
    import numpy as np
    import concourse.bacc as bacc
    from concourse import mybir
    from concourse.bass_utils import run_bass_kernel_spmd as run

    f = np.float32
    a = {k: np.ascontiguousarray(v) for k, v in inputs.items()}

    def chan(v):
        return v.reshape(-1, v.shape[-1] // P, P).transpose(2, 0, 1).reshape(P, -1)

    def used_order(v):
        return np.concatenate([v[CONV:], v[:CONV]])

    ln_g = [a["ln_in_g"]] + [a[f"ln{j}_g"][l] for l in range(DEPTH) for j in (1, 2)]
    ln_b = [a["ln_in_b"]] + [a[f"ln{j}_b"][l] for l in range(DEPTH) for j in (1, 2)]
    params = np.concatenate([np.concatenate([
        chan(ln_g[2 * l]), chan(ln_b[2 * l]), chan(ln_g[2 * l + 1]), chan(ln_b[2 * l + 1]), chan(a["conv_a"][l]),
        chan(a["pool_scale"][l]), chan(used_order(a["mix_norm_g"][l])), chan(a["ffn_conv_w"][l]),
        chan(a["ffn_conv_b"][l])], axis=1) for l in range(DEPTH)])
    small_w = np.concatenate([np.concatenate([a["fourier_w"][l], a["pool_w"][l]]).transpose(1, 0, 2).reshape(P, -1)
                              for l in range(DEPTH)])
    ln_rows = np.stack([v for g, b in zip(ln_g, ln_b) for v in (g, b)])

    c, t = np.arange(P), np.arange(S)
    ang_c = 2 * np.pi * (np.outer(c, c) % P) / P
    ang_t = 2 * np.pi * (np.outer(t, t) % S) / S
    dft_c = np.concatenate([np.cos(ang_c), np.sin(ang_c)], axis=1) / np.sqrt(P)
    dft_t = np.concatenate([m[parity::2, :P] for parity in range(2) for m in (np.cos(ang_t), -np.sin(ang_t))],
                           axis=1) / np.sqrt(S)
    inv = np.stack([1.0 / (np.minimum(t + h, S) - np.maximum(t - h, 0)) for h in POOL_HALF]).reshape(1, -1)
    consts = np.concatenate([np.eye(P), np.full((P, 1), 1 / POOLW), np.full((P, 1), 1 / CONV), dft_c,
                             np.broadcast_to(inv, (P, 4 * S)), dft_t], axis=1).astype(f)

    arrays = {"x": a["x"], "w_in": a["w_in"], "w_out": a["w_out"], "w_gate": a["w_gate"], "w_up": a["w_up"],
              "w_down": a["w_down"], "params": params, "small_w": small_w, "ln_rows": ln_rows, "consts": consts}
    nc = bacc.Bacc("TRN2", target_bir_lowering=False, num_devices=1)
    arrays = {k: np.ascontiguousarray(v) for k, v in arrays.items()}
    args = [nc.dram_tensor(k, v.shape, mybir.dt.from_np(v.dtype), kind="ExternalInput").ap() for k, v in arrays.items()]
    out = nc.dram_tensor("out", (1, S, D), mybir.dt.float32, kind="ExternalOutput").ap()
    build(nc, *args, out)
    return run(nc, [arrays], core_ids=[0]).results[0]["out"]
```
